# Optimizing a Trainium2 kernel written in Bass

```python
import jax, jax.numpy as jnp
from jax import lax
import numpy as np

D_MODEL = 2048
BATCH = 1
SEQ = 128
DEPTH = 2
DEC_BATCH = 1
DEC_SEQ = 256
PAST_LEN = 128

GRID_W = 64
HEAD_DIM = 128
N_Q_HEADS = 12
N_KV_HEADS = 4
Q_PER_KV = N_Q_HEADS // N_KV_HEADS
ATTN_WIDTH = N_Q_HEADS * HEAD_DIM
KV_WIDTH = N_KV_HEADS * HEAD_DIM
WINDOW = 128
BLOCK = 128
ROPE_THETA = 10000.0
FOURIER_GROUPS = 4
FOURIER_WIDTH = D_MODEL // 4
FOURIER_GROUP_DIM = FOURIER_WIDTH // FOURIER_GROUPS
POOL_WINDOWS = (2, 4, 8, 16)
POOL_WIDTH = D_MODEL // 2
POOL_GROUP_DIM = POOL_WIDTH // len(POOL_WINDOWS)
SGU_HEADS = 4
SGU_WIDTH = D_MODEL // 2
SGU_GROUP_DIM = SGU_WIDTH // SGU_HEADS
SGU_CHUNK = 128
MIX_WIDTH = ATTN_WIDTH + FOURIER_WIDTH
IN_WIDTH = 2 * ATTN_WIDTH + 2 * KV_WIDTH + 2 * FOURIER_WIDTH
EVEN_SPLITS = (ATTN_WIDTH, ATTN_WIDTH + KV_WIDTH, ATTN_WIDTH + 2 * KV_WIDTH,
               2 * ATTN_WIDTH + 2 * KV_WIDTH, 2 * ATTN_WIDTH + 2 * KV_WIDTH + FOURIER_WIDTH)
ODD_SPLITS = (POOL_WIDTH, 2 * POOL_WIDTH, 2 * POOL_WIDTH + SGU_WIDTH, 2 * POOL_WIDTH + 2 * SGU_WIDTH)
N_ATTN_LAYERS = (DEPTH + 1) // 2
N_POOL_LAYERS = DEPTH // 2
EPS = 1e-6
NEG_INF = -1e30

kernel_name = "hybrid_diffusion_prefix_step"

def rmsnorm(x, g):
    x32 = x.astype(jnp.float32)
    y = x32 * lax.rsqrt(jnp.mean(x32 * x32, axis=-1, keepdims=True) + EPS)
    return (y * g.astype(jnp.float32)).astype(x.dtype)

def axial_rope_tables(t_len):
    rows = t_len // GRID_W
    row = jnp.repeat(jnp.arange(rows), GRID_W).astype(jnp.float32)
    col = jnp.tile(jnp.arange(GRID_W), rows).astype(jnp.float32)
    n_freq = HEAD_DIM // 4
    inv = ROPE_THETA ** (-jnp.arange(n_freq, dtype=jnp.float32) / n_freq)
    ang = jnp.stack([row[:, None] * inv, col[:, None] * inv], axis=1)
    return jnp.cos(ang), jnp.sin(ang)

def apply_axial_rope(x, cos, sin):
    shp = x.shape
    xr = x.reshape(shp[:-1] + (2, 2, HEAD_DIM // 4)).astype(jnp.float32)
    c = cos[None, :, None]
    s = sin[None, :, None]
    x1 = xr[..., 0, :]
    x2 = xr[..., 1, :]
    out = jnp.stack([x1 * c - x2 * s, x2 * c + x1 * s], axis=-2)
    return out.reshape(shp).astype(x.dtype)

def context_attention(q, k, v, sink):
    B, L = q.shape[:2]
    s = jnp.einsum('blhgd,bmhd->bhglm', q, k, preferred_element_type=jnp.float32) * (HEAD_DIM ** -0.5)
    sink_l = jnp.broadcast_to(sink.astype(jnp.float32)[None, :, :, None, None], s.shape[:-1] + (1,))
    p = jax.nn.softmax(jnp.concatenate([s, sink_l], axis=-1), axis=-1)[..., :-1]
    o = jnp.einsum('bhglm,bmhd->blhgd', p.astype(v.dtype), v)
    return o.reshape(B, L, ATTN_WIDTH)

def latent_window_attention(q, k, v, k_ctx, v_ctx, sink):
    B, T = q.shape[:2]
    nb = T // BLOCK
    qb = q.reshape(B, nb, BLOCK, N_KV_HEADS, Q_PER_KV, HEAD_DIM)
    pad = ((0, 0), (BLOCK, BLOCK), (0, 0), (0, 0))
    kb = jnp.pad(k, pad).reshape(B, nb + 2, BLOCK, N_KV_HEADS, HEAD_DIM)
    vb = jnp.pad(v, pad).reshape(B, nb + 2, BLOCK, N_KV_HEADS, HEAD_DIM)
    kw = jnp.concatenate([kb[:, :-2], kb[:, 1:-1], kb[:, 2:]], axis=2)
    vw = jnp.concatenate([vb[:, :-2], vb[:, 1:-1], vb[:, 2:]], axis=2)
    scale = HEAD_DIM ** -0.5
    s_loc = jnp.einsum('bnqhgd,bnkhd->bnhgqk', qb, kw, preferred_element_type=jnp.float32) * scale
    blk = jnp.arange(nb)[:, None]
    qpos = blk * BLOCK + jnp.arange(BLOCK)[None, :]
    kpos = (blk - 1) * BLOCK + jnp.arange(3 * BLOCK)[None, :]
    valid = ((jnp.abs(qpos[:, :, None] - kpos[:, None, :]) <= WINDOW)
             & (kpos >= 0)[:, None, :] & (kpos < T)[:, None, :])
    s_loc = jnp.where(valid[None, :, None, None], s_loc, NEG_INF)
    s_ctx = jnp.einsum('bnqhgd,blhd->bnhgql', qb, k_ctx, preferred_element_type=jnp.float32) * scale
    sink_l = jnp.broadcast_to(sink.astype(jnp.float32)[None, None, :, :, None, None], s_loc.shape[:-1] + (1,))
    p = jax.nn.softmax(jnp.concatenate([s_loc, s_ctx, sink_l], axis=-1), axis=-1)
    p_loc = p[..., :3 * BLOCK].astype(v.dtype)
    p_ctx = p[..., 3 * BLOCK:-1].astype(v.dtype)
    o = (jnp.einsum('bnhgqk,bnkhd->bnqhgd', p_loc, vw)
         + jnp.einsum('bnhgql,blhd->bnqhgd', p_ctx, v_ctx))
    return o.reshape(B, T, ATTN_WIDTH)

def fourier_mix(u):
    B, T, _ = u.shape
    ug = u.reshape(B, T, FOURIER_GROUPS, FOURIER_GROUP_DIM).astype(jnp.float32)
    f = jnp.fft.fft2(ug, axes=(1, 3), norm="ortho").real
    return f.reshape(B, T, FOURIER_WIDTH).astype(u.dtype)

def multiscale_pool(u, pool_w, pool_scale):
    B, T, _ = u.shape
    ug = u.reshape(B, T, len(POOL_WINDOWS), POOL_GROUP_DIM).astype(jnp.float32)
    csum = jnp.pad(jnp.cumsum(ug, axis=1), ((0, 0), (1, 0), (0, 0), (0, 0)))
    pos = jnp.arange(T)
    outs = []
    for g, w in enumerate(POOL_WINDOWS):
        lo = jnp.clip(pos - w // 2, 0, T)
        hi = jnp.clip(pos + w // 2, 0, T)
        cg = csum[:, :, g]
        cnt = (hi - lo).astype(jnp.float32)[None, :, None]
        outs.append((cg[:, hi] - cg[:, lo]) / cnt - ug[:, :, g])
    pooled = jnp.stack(outs, axis=2)
    mixed = jnp.einsum('btgc,gcd->btgd', pooled, pool_w.astype(jnp.float32))
    return (mixed.reshape(B, T, POOL_WIDTH) * pool_scale.astype(jnp.float32)).astype(u.dtype)

def spatial_gating(u, v, sgu_norm, sgu_w, sgu_b):
    B, T, _ = u.shape
    nc = T // SGU_CHUNK
    v32 = v.reshape(B, T, SGU_HEADS, SGU_GROUP_DIM).astype(jnp.float32)
    mu = jnp.mean(v32, axis=-1, keepdims=True)
    var = jnp.mean(jnp.square(v32 - mu), axis=-1, keepdims=True)
    vn = ((v32 - mu) * lax.rsqrt(var + EPS) * sgu_norm.astype(jnp.float32).reshape(SGU_HEADS, SGU_GROUP_DIM)).astype(v.dtype)
    vc = vn.reshape(B, nc, SGU_CHUNK, SGU_HEADS, SGU_GROUP_DIM)
    mixed = jnp.einsum('hpq,bnqhc->bnphc', sgu_w, vc) + sgu_b.T[None, None, :, :, None]
    return u * mixed.reshape(B, T, SGU_WIDTH)

def trunk_layer(l, x, cond, w_ada, b_ada, norm_pre, norm_post, w_in, w_out,
                attn_sink, pool_w, pool_scale, sgu_norm, sgu_w, sgu_b,
                rope, ctx_k, ctx_v):
    B, T, _ = x.shape
    j = l // 2
    mod = jax.nn.silu(cond) @ w_ada[l] + b_ada[l]
    shift, scale, gate = jnp.split(mod[:, None, :], 3, axis=-1)
    h = rmsnorm(x, norm_pre[l]) * (1 + scale) + shift
    proj = h @ w_in[l]
    k = v = None
    if l % 2 == 0:
        q, k, v, g_a, u_b, g_b = jnp.split(proj, EVEN_SPLITS, axis=-1)
        q = q.reshape(B, T, N_Q_HEADS, HEAD_DIM)
        k = k.reshape(B, T, N_KV_HEADS, HEAD_DIM)
        v = v.reshape(B, T, N_KV_HEADS, HEAD_DIM)
        sink = attn_sink[j].reshape(N_KV_HEADS, Q_PER_KV)
        if ctx_k is None:
            o_a = context_attention(q.reshape(B, T, N_KV_HEADS, Q_PER_KV, HEAD_DIM), k, v, sink)
        else:
            cos, sin = rope
            qr = apply_axial_rope(q, cos, sin).reshape(B, T, N_KV_HEADS, Q_PER_KV, HEAD_DIM)
            kr = apply_axial_rope(k, cos, sin)
            o_a = latent_window_attention(qr, kr, v, ctx_k, ctx_v, sink)
        o = jnp.concatenate([jax.nn.silu(g_a) * o_a, jax.nn.silu(g_b) * fourier_mix(u_b)], axis=-1)
    else:
        u_c, g_c, u_d, v_d, g_d = jnp.split(proj, ODD_SPLITS, axis=-1)
        o = jnp.concatenate([
            jax.nn.silu(g_c) * multiscale_pool(u_c, pool_w[j], pool_scale[j]),
            jax.nn.silu(g_d) * spatial_gating(u_d, v_d, sgu_norm[j], sgu_w[j], sgu_b[j])], axis=-1)
    x = x + gate * rmsnorm(o @ w_out[l], norm_post[l])
    return x, k, v

def setup_inputs(seed: int = 0) -> dict:
    key = jax.random.key(seed)
    ks = jax.random.split(key, 18)
    f32 = jnp.float32
    nrm = lambda k, shp: jax.random.normal(k, shp, f32)
    d_inv = D_MODEL ** -0.5
    return {
        "x_prompt": nrm(ks[0], (BATCH, SEQ, D_MODEL)),
        "x_sample": nrm(ks[1], (DEC_BATCH, DEC_SEQ, D_MODEL)),
        "cache_k": nrm(ks[2], (DEC_BATCH, N_ATTN_LAYERS, PAST_LEN, N_KV_HEADS, HEAD_DIM)),
        "cache_v": nrm(ks[3], (DEC_BATCH, N_ATTN_LAYERS, PAST_LEN, N_KV_HEADS, HEAD_DIM)),
        "c": nrm(ks[4], (DEC_BATCH, D_MODEL)),
        "c_ctx": nrm(ks[5], (D_MODEL,)),
        "w_ada": nrm(ks[6], (DEPTH, D_MODEL, 3 * D_MODEL)) * (0.5 * d_inv),
        "b_ada": nrm(ks[7], (DEPTH, 3 * D_MODEL)) * 0.02,
        "norm_pre": 1.0 + 0.02 * nrm(ks[8], (DEPTH, D_MODEL)),
        "norm_post": 1.0 + 0.02 * nrm(ks[9], (DEPTH, D_MODEL)),
        "w_in": nrm(ks[10], (DEPTH, D_MODEL, IN_WIDTH)) * d_inv,
        "w_out": nrm(ks[11], (DEPTH, MIX_WIDTH, D_MODEL)) * (MIX_WIDTH ** -0.5),
        "attn_sink": 0.5 * nrm(ks[12], (N_ATTN_LAYERS, N_Q_HEADS)),
        "pool_w": nrm(ks[13], (N_POOL_LAYERS, len(POOL_WINDOWS), POOL_GROUP_DIM, POOL_GROUP_DIM)) * (POOL_GROUP_DIM ** -0.5),
        "pool_scale": 1.0 + 0.02 * nrm(ks[14], (N_POOL_LAYERS, POOL_WIDTH)),
        "sgu_norm": 1.0 + 0.02 * nrm(ks[15], (N_POOL_LAYERS, SGU_WIDTH)),
        "sgu_w": nrm(ks[16], (N_POOL_LAYERS, SGU_HEADS, SGU_CHUNK, SGU_CHUNK)) * (SGU_CHUNK ** -0.5),
        "sgu_b": 1.0 + 0.02 * nrm(ks[17], (N_POOL_LAYERS, SGU_HEADS, SGU_CHUNK)),
    }

def reference(x_prompt, x_sample, cache_k, cache_v, c, c_ctx, w_ada, b_ada, norm_pre, norm_post,
              w_in, w_out, attn_sink, pool_w, pool_scale, sgu_norm, sgu_w, sgu_b):
    rope = axial_rope_tables(x_sample.shape[1])
    cond_ctx = c_ctx[None, :]
    xp = x_prompt
    xs = x_sample
    new_k = []
    new_v = []
    for l in range(DEPTH):
        j = l // 2
        xp, kp, vp = trunk_layer(l, xp, cond_ctx, w_ada, b_ada, norm_pre, norm_post, w_in, w_out,
                                 attn_sink, pool_w, pool_scale, sgu_norm, sgu_w, sgu_b,
                                 None, None, None)
        if l % 2 == 0:
            new_k.append(kp)
            new_v.append(vp)
            ck, cv = cache_k[:, j], cache_v[:, j]
        else:
            ck, cv = None, None
        xs, _, _ = trunk_layer(l, xs, c, w_ada, b_ada, norm_pre, norm_post, w_in, w_out,
                               attn_sink, pool_w, pool_scale, sgu_norm, sgu_w, sgu_b,
                               rope, ck, cv)
    new_cache_k = jnp.stack(new_k, axis=1)
    new_cache_v = jnp.stack(new_v, axis=1)
    return (xp, xs, new_cache_k, new_cache_v)


_drawn_inputs = setup_inputs


def setup_inputs(seed=0):
    import zlib

    import numpy as np

    out = dict(_drawn_inputs(seed))
    spreads = {}
    factors = {'norm_pre': 2.951,
     'norm_post': 6.972,
     'attn_sink': 64.0,
     'pool_scale': 64.0,
     'sgu_norm': 58.352,
     'sgu_b': 61.271,
     'cache_k': 8.0,
     'cache_v': 8.0}
    for name, (base, spread) in spreads.items():
        noise = np.random.default_rng([zlib.crc32(name.encode()), seed]).standard_normal(out[name].shape)
        drawn = base * np.exp(spread * noise) if base else spread * noise
        out[name] = __import__('jax').numpy.asarray(drawn.astype(out[name].dtype))
    for name, factor in factors.items():
        out[name] = (out[name] * factor).astype(out[name].dtype)
    return out
```

```python
from contextlib import ExitStack

import concourse.bass as bass
from concourse import mybir

F32 = mybir.dt.float32
F32R = mybir.dt.float32r
ALU = mybir.AluOpType
ACT = mybir.ActivationFunctionType
AX = mybir.AxisListType

P = 128
D = 2048
TOKS = 3
NT = TOKS * P
KT = D // P
CW = 512
HEADS, KV_HEADS, HD = 12, 4, 128
Q_PER_KV = HEADS // KV_HEADS
ATT = HEADS * HD
EPS = 1e-6
SCALE = HD ** -0.5
WINDOWS = (2, 4, 8, 16)
GROUP = 256

IN_CHUNKS = [
    [("k", 1536), ("v", 2048), ("q", 0), ("q", 512), ("q", 1024),
     ("ga", 2560), ("ga", 3072), ("ga", 3584), ("ub", 4096), ("gb", 4608)],
    [("uc", 0), ("uc", 512), ("vd", 3072), ("vd", 3584), ("gc", 1024), ("gc", 1536),
     ("ud", 2048), ("ud", 2560), ("gd", 4096), ("gd", 4608)],
]
N_IN = len(IN_CHUNKS[0])
N_OUT = D // CW
PER_LAYER = N_IN + N_OUT
CHUNKS = [(layer, kind, col) for layer in range(2)
          for kind, col in IN_CHUNKS[layer] + [("out", CW * j) for j in range(N_OUT)]]
NTH = [sum(x[:2] == CHUNKS[c][:2] for x in CHUNKS[:c]) for c in range(len(CHUNKS))]
ROPED = {"k": 0, "q": 1}
GATED = {"ga": 0, "gb": ATT, "gc": 0, "gd": 1024}
L1 = PER_LAYER
SHIFT_COL, SCALE_COL, GATE_COL = 0, 1, 2
BLOCKS = [(0, SCALE_COL), (0, SHIFT_COL), (0, GATE_COL), (1, SCALE_COL), (1, SHIFT_COL), (1, GATE_COL)]
GATE_BLOCK = (2, 5)
SCALE_BLOCK = (0, 3)
SHIFT_BLOCK = (1, 4)
NORM_BLOCKS = [0, 2, 3, 5]
SEAM_ADA = 6
WRING = 3
RAW = 3


def head_units():
    return [(g, t, h) for g in range(HEADS // 4) for t in range(TOKS) for h in range(4)]


def timetable():
    at = {}

    def put(c, s, *entry):
        c, s = c + s // KT, s % KT
        at.setdefault(("at", c, s), []).append(entry)

    def pre(c, *entry):
        at.setdefault(("pre", c), []).append(entry)

    for m in (0, 1):
        pre(0, "cols", m)
    for first in (0, L1):
        layer = first // L1
        if layer:
            for n in range(2):
                pre(L1, "gate_y", L1 - 1, n)
            pre(L1, "residual", 0)
            pre(L1, "ada", 5, 0, SEAM_ADA)
        for k in range(3):
            pre(first, "h", layer, k)
        for k in range(3, KT):
            put(first, k - 3, "h", layer, k)
    for c, (layer, kind, _) in enumerate(CHUNKS):
        nxt = c + 1
        if kind == "out":
            if c in (L1 - 1, 2 * L1 - 1):
                continue
            for n in range(2):
                put(nxt, n, "gate_y", c, n)
            continue
        step = {"k": 3, "q": 3, "vd": 2}.get(kind, 1)
        for t in range(TOKS):
            put(nxt, step * t, "evac", c, t)
            if kind in ROPED:
                put(nxt, step * t + 2, "turn", c, t)
            if kind == "vd":
                put(nxt, step * t + 1, "evac2", c, t)
                put(nxt, step * t + 5, "mix", c, t)
    first = 3 * KT + 4
    for u in range(HEADS * TOKS):
        put(0, first + 2 * u + 2, "turn_p", u)
        put(0, first + 2 * u + 3, "pv", u)
    for u in range(HEADS * TOKS):
        put(0, first + 2 * u, "scores", u)
    for g in range(HEADS // 4):
        put(0, first + 2 * (12 * g + 11) + 4, "denominator", g)
    for k in range(8):
        put(8, k, "o", 0, k)
        put(L1 + 5 + k // 4, 6 + k % 4, "o", 1, k)
        for layer in range(2):
            put(layer * L1 + N_IN, k + 1, "o", layer, 8 + k)
    for g in range(4):
        put(9, 3 + 3 * g, "dft_ctx", g)
        put(9, 4 + 3 * g, "dft_lat", g)
        put(9, 5 + 3 * g, "dft_ch", g)
        c, s = L1 + 1 + g // 2, 4 + 4 * (g % 2)
        for j in range(2):
            put(c, s + j, "pool", g, j)
            put(c, s + 2 + j, "pool_mix", g, j)
    rows = [(m, k) for m in (2, 3, 4) for k in range(KT)]
    for n, (m, k) in enumerate(rows):
        put(n // 4, 4 * (n % 4) + 3, "ada", m, k, 1)
    for n, k in enumerate(range(SEAM_ADA, KT)):
        put(L1 + n // 4, 4 * (n % 4) + 3, "ada", 5, k, 1)
    put(8, 1, "cols", 3)
    put(12, 1, "cols", 4)
    end = len(CHUNKS)
    for n in range(2):
        pre(end, "gate_y", end - 1, n)
    pre(end, "residual", 1)
    return at


SIDE = {"cols", "h", "gate_y", "ada", "turn", "turn_p", "pv", "scores", "o", "dft_ctx", "dft_lat",
        "dft_ch", "pool", "pool_mix", "mix"}


def places():
    for c in range(len(CHUNKS) + 1):
        yield ("pre", c)
        if c < len(CHUNKS):
            for s in range(KT):
                yield ("at", c, s)


def hybrid_step(nc, x_prompt, x_sample, cond_cols, w_ada, ada_rows, norm_rows, w_in, w_out, cache_kt,
                cache_v, sink_units, pool_w, pool_scale, sgu_norm, sgu_wt, sgu_bt,
                identity, row_select, rope, window_mask, dft, pool_mats,
                y_prompt, y_sample, new_k, new_v):
    table = timetable()
    side = [e for p in places() for e in table.get(p, ()) if e[0] in SIDE]
    nth_side = {e: n for n, e in enumerate(side)}
    assert len(nth_side) == len(side)

    loads = [("ada", m, k) for m in (0, 1) for k in range(KT)] + [("mm", 0)]
    for p in places():
        if p[0] == "at" and p[2] % 4 == 0 and 4 * p[1] + p[2] // 4 + 1 < 4 * len(CHUNKS):
            loads.append(("mm", 4 * p[1] + p[2] // 4 + 1))
        loads += [("ada", e[1], e[2] + i) for e in table.get(p, ()) if e[0] == "ada" for i in range(e[3])]
    nth_load = {x: n for n, x in enumerate(loads)}
    ada_entry = {(e[1], e[2] + i): e for e in side if e[0] == "ada" for i in range(e[3])}
    early = [("ada", m, k) for m in (0, 1) for k in range(KT)]
    early += [("ada", e[1], e[2] + i) for e in side if e[0] == "ada" for i in range(e[3] - 1)]

    with ExitStack() as ctx:
        place = [(nc.sbuf_base + 63) // 64 * 64]

        def tensor(name, shape, dt=F32, at=None):
            size = 4
            for n in shape:
                size *= n
            if at is None:
                at = place[0]
                place[0] += (size + 31) // 32 * 32
            return nc.alloc_sbuf_tensor_at(name, [P, *shape], dt, offset=at)

        x = tensor("x", [TOKS, D])
        mixed = tensor("mixed", [TOKS, D])
        h_op = tensor("h_op", [2, KT, NT], F32R)
        region = place[0]
        qk_t = tensor("qk_t", [16, NT])
        u_pool = tensor("u_pool", [TOKS, 1024], at=region)
        pooled = tensor("pooled", [8, NT], at=region + 4 * TOKS * 1024)
        o_low = tensor("o_low", [2, 8, NT], F32R, at=region)
        raw = tensor("raw", [RAW, D])
        w_hi = tensor("w_hi", [WRING, 2, CW], F32R)
        w_lo = tensor("w_lo", [WRING, 2, CW], F32R)
        ident = tensor("ident", [P])
        row_sel = tensor("row_sel", [2, P])
        cond = tensor("cond", [KT, 32])
        cond_in = tensor("cond_in", [KT, 2])
        scale_t = tensor("scale_t", [4, P])
        shift_t = tensor("shift_t", [4, P])
        rows = tensor("rows", [CW])
        gate = tensor("gate", [CW])
        bias_rows = tensor("bias_rows", [CW])
        weight_rows = tensor("weight_rows", [CW])
        silu = tensor("silu", [2, CW])
        sinks = tensor("sinks", [36])
        neg_sinks = tensor("neg_sinks", [36])
        row_max = tensor("row_max", [36])
        neg_max = tensor("neg_max", [36])
        row_sum = tensor("row_sum", [36])
        sink_exp = tensor("sink_exp", [36])
        inv_sum = tensor("inv_sum", [36])
        sq = tensor("sq", [TOKS, 4])
        stat = tensor("stat", [8, TOKS])
        ln_stats = tensor("ln_stats", [2, 6])
        ln_mv = tensor("ln_mv", [2, 2])
        ln_std = tensor("ln_std", [2])
        area = place[0]

        def in_area(name, shape, at):
            return tensor(name, shape, at=area + 4 * at)

        v_nat = in_area("v_nat", [TOKS, CW], 0)
        cache_k_sb = in_area("cache_k_sb", [KV_HEADS, P], 1536)
        cache_v_sb = in_area("cache_v_sb", [CW], 2048)
        rope_sb = in_area("rope_sb", [2, 2, P], 2560)
        mask_sb = in_area("mask_sb", [2, P], 3072)
        probs = in_area("probs", [NT], 3328)
        probs_t = in_area("probs_t", [NT], 3712)
        dft_sb = in_area("dft_sb", [1536], 1536)
        dft_c = in_area("dft_c", [256], 3328)
        dft_l = in_area("dft_l", [CW], 3584)
        roped = in_area("roped", [CW], 4168)
        junk = in_area("junk", [CW], 4168)
        pool_m = in_area("pool_m", [1600], 0)
        pool_s = in_area("pool_s", [1024], 1600)
        pool_w_sb = in_area("pool_w_sb", [2, 2, GROUP], 2624)
        sgu_w_sb = in_area("sgu_w_sb", [4, P], 3648)
        sgu_b_sb = in_area("sgu_b_sb", [4], 4160)
        v_normed = in_area("v_normed", [TOKS, CW], 0)
        sgu_n = in_area("sgu_n", [1024], 1536)
        assert area + 4 * 4680 <= nc.sbuf_usable_end, (area + 4 * 4680, nc.sbuf_usable_end)
        rope_tmp = silu[:, 0, :]
        h_tmp = silu[:, 0, 0:NT]
        dft_128 = dft_sb[:, 0:256]
        dft_256 = dft_sb[:, 256:1280].rearrange("p (a n) -> p a n", a=2)
        dft_chan = dft_sb[:, 1280:1536]
        pool_ctx = pool_m[:, 0:512].rearrange("p (g n) -> p g n", g=4)
        pool_own = pool_m[:, 512:1536].rearrange("p (a g n) -> p a g n", a=2, g=4)
        pool_cross = pool_m[:, 1536:1600].rearrange("p (a g n) -> p a g n", a=2, g=4)

        bank = [ctx.enter_context(nc.psum_tensor(f"bank{i}", [P, CW], F32)) for i in range(8)]

        def acc(c, t):
            return bank[3 * (c % 2) + t]

        def sem(name):
            return ctx.enter_context(nc.semaphore(name))

        raw_in = [sem(f"raw_in{i}") for i in range(RAW)]
        const_in = sem("const_in")
        cond_landed = sem("cond_landed")
        x_in = sem("x_in")
        attn_in = sem("attn_in")
        bias_in = sem("bias_in")
        weight_in = sem("weight_in")
        dft_in = sem("dft_in")
        pool_in = sem("pool_in")
        pool_w_in = [sem("pool_w_in0"), sem("pool_w_in1")]
        sgu_in = sem("sgu_in")
        stored = sem("stored")
        k_stored = sem("k_stored")
        v_stored = sem("v_stored")
        cleared = sem("cleared")
        cond_ready = sem("cond_ready")
        ada_done = sem("ada_done")
        hi_ready = sem("hi_ready")
        lo_ready = sem("lo_ready")
        mm_done = sem("mm_done")
        acc_free = [sem("acc_free0"), sem("acc_free1")]
        side_full = [sem("side_full0"), sem("side_full1")]
        side_free = [sem("side_free0"), sem("side_free1")]
        bias_used = sem("bias_used")
        rows_done = sem("rows_done")
        op_hi = sem("op_hi")
        roped_ready = sem("roped_ready")
        neg_max_ready = sem("neg_max_ready")
        sink_shifted = sem("sink_shifted")
        sink_exped = sem("sink_exped")
        inv_ready = sem("inv_ready")
        silu_ready = sem("silu_ready")
        y_squared = sem("y_squared")
        y_mean = sem("y_mean")
        y_root = sem("y_root")
        x_ready = sem("x_ready")
        x_squared = sem("x_squared")
        x_mean = sem("x_mean")
        x_root = sem("x_root")
        xn_ready = sem("xn_ready")
        ln_var_ready = sem("ln_var_ready")
        ln_root = sem("ln_root")
        vn_ready = sem("vn_ready")
        act_own = sem("act_own")
        dve_own = sem("dve_own")

        def side_bank(e):
            return bank[6 + nth_side[e] % 2]

        def wait_full(eng, *e):
            eng.wait_ge(side_full[nth_side[e] % 2], nth_side[e] // 2 + 1)

        def wait_free(eng, *e):
            eng.wait_ge(side_free[nth_side[e] % 2], nth_side[e] // 2 + 1)

        def filled(ins, e):
            ins.then_inc(side_full[nth_side[e] % 2], 1)

        def freed(ins, e):
            ins.then_inc(side_free[nth_side[e] % 2], 1)

        def wait_acc(eng, c, t):
            if CHUNKS[c][1] in ROPED:
                eng.wait_ge(roped_ready, nth_roped[c, t] + 1)
            else:
                before = sum(CHUNKS[b][1] not in ROPED for b in range(c % 2, c, 2))
                eng.wait_ge(acc_free[c % 2], TOKS * before + t + 1)

        def wait_chunk(eng, c):
            eng.wait_ge(mm_done, 8 * (c + 1))

        def wait_load(eng, *what):
            n = nth_load[what]
            eng.wait_ge(raw_in[n % RAW], 16 * (n // RAW + 1))

        def nth_op(kind, layer, k):
            return 2 * KT * layer + (KT if kind == "o" else 0) + k

        units = head_units()
        gate_chunks = [(c, t) for c in range(len(CHUNKS)) if CHUNKS[c][1] in GATED for t in range(TOKS)]
        nth_gate = {ct: n for n, ct in enumerate(gate_chunks)}
        roped_chunks = [c for c in range(len(CHUNKS)) if CHUNKS[c][1] in ROPED]
        nth_roped = {(c, t): TOKS * n + t for n, c in enumerate(roped_chunks) for t in range(TOKS)}
        out_chunks = [c for c in range(len(CHUNKS)) if CHUNKS[c][1] == "out"]
        nth_out = {c: n for n, c in enumerate(out_chunks)}
        first_q = roped_chunks[1]
        v_chunk = next(c for c in range(len(CHUNKS)) if CHUNKS[c][1] == "v")
        ub_chunk = next(c for c in range(len(CHUNKS)) if CHUNKS[c][1] == "ub")
        uc_chunks = [c for c in range(len(CHUNKS)) if CHUNKS[c][1] == "uc"]
        vd_chunks = [c for c in range(len(CHUNKS)) if CHUNKS[c][1] == "vd"]

        def gate_of(layer, k):
            kinds = (("ga", "gb"), ("gc", "gd"))[layer]
            col = k * P
            for c, (at_layer, kind, _) in enumerate(CHUNKS):
                if at_layer == layer and kind in kinds and GATED[kind] + CW * NTH[c] == col // CW * CW:
                    return c

        block = ctx.enter_context(nc.Block())

        @block.sync
        def _(sp):
            for n, what in enumerate(loads):
                if n >= RAW:
                    old = loads[n - RAW]
                    if old[0] == "mm":
                        sp.wait_ge(lo_ready, 2 * old[1] + 2)
                    elif old in early:
                        sp.wait_ge(ada_done, early.index(old) + 1)
                    else:
                        wait_full(sp, *ada_entry[old[1:]])
                slot = raw[:, n % RAW, :]
                if what[0] == "ada":
                    layer, third = BLOCKS[what[1]]
                    src = w_ada[layer, what[2] * P:(what[2] + 1) * P, third * D:(third + 1) * D]
                    sp.dma_start(slot, src).then_inc(raw_in[n % RAW], 16)
                else:
                    c, quarter = divmod(what[1], 4)
                    layer, kind, col = CHUNKS[c]
                    w = (w_out if kind == "out" else w_in)[layer].rearrange("(k p) n -> p k n", p=P)
                    sp.dma_start(slot.rearrange("p (k n) -> p k n", n=CW),
                                 w[:, 4 * quarter:4 * quarter + 4, col:col + CW])\
                        .then_inc(raw_in[n % RAW], 16)
            for t in range(TOKS):
                sp.wait_ge(x_ready, TOKS + t + 1)
                dst = y_prompt[0] if t == 0 else y_sample[0, (t - 1) * P:t * P, :]
                sp.dma_start(dst, x[:, t, :]).then_inc(stored, 16)
            sp.wait_ge(stored, 16 * TOKS)
            sp.wait_ge(k_stored, 16)
            sp.wait_ge(v_stored, 16)

        @block.gpsimd
        def _(pool):
            pool.memset(cond[:, :, :], 0.0).then_inc(cleared, 1)

            def load_bias(m):
                if m in (1, 2):
                    pool.wait_ge(bias_used, m)
                elif m:
                    wait_free(pool, *ada_entry[m - 1, 0])
                pool.dma_start(bias_rows[:, :], ada_rows[m]).then_inc(bias_in, 16)

            def load_weight(n):
                if n:
                    pool.wait_ge(rows_done, n)
                pool.dma_start(weight_rows[:, :], norm_rows[n]).then_inc(weight_in, 16)

            def load_pool_w(g):
                if g >= 2:
                    wait_full(pool, "pool_mix", g - 2, 1)
                pool.dma_start(pool_w_sb[:, g % 2, :, :],
                               pool_w[0, g].rearrange("(a p) n -> p a n", p=P))\
                    .then_inc(pool_w_in[g % 2], 16)

            pool.dma_start(ident[:, :], identity).then_inc(const_in, 16)
            load_bias(0)
            load_weight(0)
            pool.dma_start(row_sel[:, :, :], row_select).then_inc(const_in, 16)
            pool.dma_start(rope_sb[:, :, :, :], rope).then_inc(attn_in, 16)
            pool.dma_start(mask_sb[:, :, :], window_mask).then_inc(attn_in, 16)
            pool.dma_start(cache_k_sb[:, :, :], cache_kt).then_inc(attn_in, 16)
            pool.dma_start(cache_v_sb[:, :], cache_v).then_inc(attn_in, 16)
            pool.dma_start(sinks[:, :], sink_units.partition_broadcast(P)).then_inc(attn_in, 16)
            load_bias(1)
            load_bias(2)
            load_weight(1)
            pool.wait_ge(roped_ready, 1)
            pool.dma_start(new_k, roped[:, :]).then_inc(k_stored, 16)
            load_bias(3)
            wait_acc(pool, v_chunk, 0)
            pool.dma_start(new_v, v_nat[:, 0, :]).then_inc(v_stored, 16)
            load_weight(2)
            load_bias(4)
            load_weight(3)
            wait_full(pool, "pv", len(units) - 1)
            pool.dma_start(dft_sb[:, :], dft).then_inc(dft_in, 16)
            load_bias(5)
            wait_full(pool, "dft_ch", 3)
            pool.dma_start(pool_m[:, :], pool_mats).then_inc(pool_in, 16)
            pool.dma_start(pool_s[:, :], pool_scale.partition_broadcast(P)).then_inc(pool_in, 16)
            pool.dma_start(sgu_w_sb[:, :, :], sgu_wt).then_inc(pool_in, 16)
            pool.dma_start(sgu_b_sb[:, :], sgu_bt).then_inc(pool_in, 16)
            for g in range(4):
                load_pool_w(g)
            wait_free(pool, "pool_mix", 3, 1)
            wait_free(pool, "pool_mix", 3, 0)
            pool.dma_start(sgu_n[:, :], sgu_norm.partition_broadcast(P)).then_inc(sgu_in, 16)

        @block.tensor
        def _(pe):
            def ada_products(dst, m, k, start, stop):
                n = nth_load[("ada", m, k)]
                wait_load(pe, "ada", m, k)
                for j in range(4):
                    last = pe.matmul(dst[32 * j:32 * j + 32, :], cond[:, k, :],
                                     raw[:, n % RAW, CW * j:CW * (j + 1)],
                                     start=start, stop=stop)
                return last

            def operand(layer, kind, part, k, t):
                src = o_low if kind == "out" and k < 8 else h_op
                return src[:, part, k, t * P:(t + 1) * P]

            def k_step(c, k):
                layer, kind, _ = CHUNKS[c]
                if k == 0 and c >= 2:
                    wait_acc(pe, c - 2, TOKS - 1)
                half = 8 * c + k // 2
                if k % 2 == 0:
                    pe.wait_ge(lo_ready, half + 1)
                if c in (0, L1):
                    wait_free(pe, "h", layer, k)
                if c in (N_IN, L1 + N_IN):
                    wait_free(pe, "o", layer, k)
                hi = w_hi[:, half % WRING, k % 2, :]
                lo = w_lo[:, half % WRING, k % 2, :]
                for t in range(TOKS):
                    out = acc(c, t)[:, :]
                    pe.matmul(out, operand(layer, kind, 0, k, t), hi, start=k == 0, stop=False)
                    pe.matmul(out, operand(layer, kind, 0, k, t), lo, start=False, stop=False)
                    last = pe.matmul(out, operand(layer, kind, 1, k, t), hi, start=False, stop=k == KT - 1)
                if k % 2:
                    last.then_inc(mm_done, 1)

            def side_product(e):
                n = nth_side[e]
                out = side_bank(e)
                what = e[0]
                if n >= 2:
                    pe.wait_ge(side_free[n % 2], n // 2)
                if what == "ada":
                    m, k0, count = e[1:]
                    for k in range(k0, k0 + count):
                        last = ada_products(out, m, k, k == k0, k == k0 + count - 1)
                        if k < k0 + count - 1:
                            last.then_inc(ada_done, 1)
                elif what == "cols":
                    if e[1] in NORM_BLOCKS:
                        pe.wait_ge(rows_done, NORM_BLOCKS.index(e[1]) + 1)
                    elif e[1] == SHIFT_BLOCK[0]:
                        pe.wait_ge(bias_used, 2)
                    else:
                        wait_free(pe, *ada_entry[e[1], KT - 1])
                    src = gate if e[1] == SHIFT_BLOCK[0] else rows
                    for i in range(4):
                        last = pe.transpose(out[:, i * P:(i + 1) * P], src[:, i * P:(i + 1) * P], ident[:, :])
                elif what == "h":
                    layer, k = e[1:]
                    if k == 0:
                        pe.wait_ge(xn_ready, TOKS * (layer + 1))
                    for t in range(TOKS):
                        last = pe.transpose(out[:, t * P:(t + 1) * P], mixed[:, t, k * P:(k + 1) * P], ident[:, :])
                elif what == "o":
                    layer, k = e[1:]
                    wait_acc(pe, gate_of(layer, k), TOKS - 1)
                    for t in range(TOKS):
                        last = pe.transpose(out[:, t * P:(t + 1) * P], mixed[:, t, k * P:(k + 1) * P], ident[:, :])
                elif what == "gate_y":
                    c, n_cond = e[1:]
                    layer, _, col = CHUNKS[c]
                    j = col // CW
                    pe.wait_ge(rows_done, NORM_BLOCKS.index(GATE_BLOCK[layer]) + 1)
                    last = pe.matmul(out[:, :], row_sel[32 * j:32 * j + 32, n_cond, :],
                                     gate[32 * j:32 * j + 32, :], start=True, stop=True)
                elif what == "turn":
                    c, t = e[1:]
                    pe.wait_ge(roped_ready, nth_roped[c, t] + 1)
                    for h in range(4):
                        last = pe.transpose(out[:, h * P:(h + 1) * P], roped[:, h * P:(h + 1) * P], ident[:, :])
                elif what == "scores":
                    g, t, i = units[e[1]]
                    h = 4 * g + i
                    kv = h // Q_PER_KV
                    wait_free(pe, "turn", first_q + g, t)
                    for s in range(1 if t == 0 else TOKS):
                        wait_free(pe, "turn", roped_chunks[0], s)
                    q = qk_t[:, h, t * P:(t + 1) * P]
                    if t == 0:
                        last = pe.matmul(out[:, 0:P], q, qk_t[:, HEADS + kv, 0:P], start=True, stop=True)
                    else:
                        pe.wait_ge(attn_in, 16 * 5)
                        pe.matmul(out[:, 0:2 * P], q, qk_t[:, HEADS + kv, P:NT], start=True, stop=True)
                        last = pe.matmul(out[:, 2 * P:NT], q, cache_k_sb[:, kv, :], start=True, stop=True)
                elif what == "turn_p":
                    u = e[1]
                    wait_free(pe, "scores", u)
                    for s in range(1 if units[u][1] == 0 else TOKS):
                        last = pe.transpose(out[:, s * P:(s + 1) * P], probs[:, s * P:(s + 1) * P], ident[:, :])
                elif what == "pv":
                    u = e[1]
                    g, t, i = units[u]
                    kv = (4 * g + i) // Q_PER_KV
                    wait_free(pe, "turn_p", u)
                    wait_acc(pe, v_chunk, TOKS - 1)
                    vs = slice(kv * HD, (kv + 1) * HD)
                    values = [v_nat[:, 0, vs]] if t == 0 else [v_nat[:, 1, vs], v_nat[:, 2, vs], cache_v_sb[:, vs]]
                    for s, v in enumerate(values):
                        last = pe.matmul(out[:, 0:HD], probs_t[:, s * P:(s + 1) * P], v,
                                         start=s == 0, stop=s == len(values) - 1)
                elif what == "dft_ctx":
                    ch = slice(e[1] * P, (e[1] + 1) * P)
                    wait_acc(pe, ub_chunk, 0)
                    pe.wait_ge(dft_in, 16)
                    last = pe.matmul(out[:, 0:256], v_nat[:, 0, ch], dft_128, start=True, stop=True)
                elif what == "dft_lat":
                    ch = slice(e[1] * P, (e[1] + 1) * P)
                    wait_acc(pe, ub_chunk, TOKS - 1)
                    for a in range(2):
                        last = pe.matmul(out[:, :], v_nat[:, 1 + a, ch], dft_256[:, a, :], start=a == 0, stop=a == 1)
                elif what == "dft_ch":
                    wait_free(pe, "dft_ctx", e[1])
                    wait_free(pe, "dft_lat", e[1])
                    pairs = [(dft_c[:, 0:P], dft_c[:, P:2 * P])]
                    pairs += [(dft_l[:, a * P:(a + 1) * P], dft_l[:, (2 + a) * P:(3 + a) * P]) for a in range(2)]
                    for t, (cos_part, sin_part) in enumerate(pairs):
                        o = out[:, t * P:(t + 1) * P]
                        pe.matmul(o, cos_part, dft_chan[:, 0:P], start=True, stop=False)
                        last = pe.matmul(o, sin_part, dft_chan[:, P:2 * P], start=False, stop=True)
                elif what == "pool":
                    g, j = e[1:]
                    ch = slice(g * GROUP + j * P, g * GROUP + (j + 1) * P)
                    wait_acc(pe, uc_chunks[g // 2], TOKS - 1)
                    pe.wait_ge(pool_in, 16 * 4)
                    pe.matmul(out[:, 0:P], u_pool[:, 0, ch], pool_ctx[:, g, :], start=True, stop=True,
                              skip_group_check=True)
                    pe.matmul(out[:, P:2 * P], u_pool[:, 1, ch], pool_own[:, 0, g, :], start=False, stop=True,
                              skip_group_check=True)
                    pe.matmul(out[:, 2 * P:NT], u_pool[:, 2, ch], pool_own[:, 1, g, :], start=False, stop=True,
                              skip_group_check=True)
                    pe.matmul(out[:, 2 * P:2 * P + 8], u_pool[:, 1, ch], pool_cross[:, 0, g, :],
                              start=False, stop=True, skip_group_check=True)
                    last = pe.matmul(out[:, 2 * P - 8:2 * P], u_pool[:, 2, ch], pool_cross[:, 1, g, :],
                                     start=False, stop=True, skip_group_check=True)
                elif what == "pool_mix":
                    g, part = e[1:]
                    pe.wait_ge(pool_w_in[g % 2], 16 * (g // 2 + 1))
                    for j in range(2):
                        wait_free(pe, "pool", g, j)
                    for i, t in enumerate((0, 1) if part == 0 else (2,)):
                        for j in range(2):
                            last = pe.matmul(out[:, i * GROUP:(i + 1) * GROUP],
                                             pooled[:, 2 * g + j, t * P:(t + 1) * P],
                                             pool_w_sb[:, g % 2, j, :], start=j == 0, stop=j == 1)
                elif what == "mix":
                    c, t = e[1:]
                    pe.wait_ge(vn_ready, TOKS * NTH[c] + t + 1)
                    for i in range(2):
                        last = pe.matmul(out[:, i * GROUP:(i + 1) * GROUP], sgu_w_sb[:, 2 * NTH[c] + i, :],
                                         v_normed[:, t, i * GROUP:(i + 1) * GROUP], start=True, stop=True)
                filled(last, e)

            pe.wait_ge(cond_ready, 1)
            for m in (0, 1):
                for k in range(KT):
                    ada_products(bank[3 + m], m, k, k == 0, k == KT - 1).then_inc(ada_done, 1)
            pe.wait_ge(const_in, 32)
            for p in places():
                if p[0] == "at":
                    k_step(p[1], p[2])
                for e in table.get(p, ()):
                    if e[0] in SIDE:
                        side_product(e)

        @block.scalar
        def _(act):
            own = [0]

            def then_own(ins):
                own[0] += 1
                ins.then_inc(act_own, 1)
                act.wait_ge(act_own, own[0])

            def round_half(half):
                wait_load(act, "mm", half // 2)
                if half >= WRING:
                    act.wait_ge(mm_done, half - WRING + 1)
                n = nth_load["mm", half // 2]
                src = raw[:, n % RAW, (half % 2) * 2 * CW:(half % 2 + 1) * 2 * CW]
                act.activation(w_hi[:, half % WRING, :, :].rearrange("p k n -> p (k n)"), src, ACT.Copy)\
                    .then_inc(hi_ready, 1)

            def norm_x(layer):
                for t in range(TOKS):
                    if layer == 0:
                        if t == 0:
                            act.wait_ge(x_in, 16 * TOKS)
                    else:
                        act.wait_ge(x_ready, t + 1)
                    act.activation(mixed[:, t, :], x[:, t, :], ACT.Square, accum_out=stat[:, 4, t:t + 1])\
                        .then_inc(x_squared, 1)
                act.wait_ge(x_mean, layer + 1)
                act.activation(stat[:, 6, :], stat[:, 5, :], ACT.Sqrt).then_inc(x_root, 1)

            def residual_root(layer):
                act.wait_ge(y_mean, layer + 1)
                act.activation(stat[:, 2, :], stat[:, 1, :], ACT.Sqrt).then_inc(y_root, 1)

            def square_y(c):
                wait_chunk(act, c)
                j = CHUNKS[c][2] // CW
                for t in range(TOKS):
                    n = TOKS * nth_out[c] + t
                    if n:
                        act.wait_ge(y_squared, n)
                    act.activation(junk[:, :], acc(c, t)[:, :], ACT.Square, accum_out=sq[:, t, j:j + 1])\
                        .then_inc(y_squared, 1)
                    act.activation(mixed[:, t, CW * j:CW * (j + 1)], acc(c, t)[:, :], ACT.Copy)\
                        .then_inc(acc_free[c % 2], 1)

            def part(e):
                what = e[0]
                if what == "cols":
                    wait_full(act, *e)
                    dst = scale_t if e[1] in SCALE_BLOCK else shift_t
                    freed(act.activation(dst[:, :, :].rearrange("p a n -> p (a n)"), side_bank(e)[:, :], ACT.Copy), e)
                elif what == "h":
                    layer, k = e[1:]
                    j, i = divmod(k, 4)
                    if k == 0:
                        wait_free(act, "cols", SCALE_BLOCK[layer])
                        wait_free(act, "cols", SHIFT_BLOCK[layer])
                    wait_full(act, *e)
                    for c_, lo_, hi_ in ((0, 0, P), (1, P, NT)):
                        col = 32 * j + c_
                        last = act.activation(h_op[:, 0, k, lo_:hi_], side_bank(e)[:, lo_:hi_], ACT.Identity,
                                              bias=shift_t[:, i, col:col + 1], scale=scale_t[:, i, col:col + 1])
                    last.then_inc(op_hi, 1)
                elif what == "o":
                    layer, k = e[1:]
                    wait_full(act, *e)
                    dst = (o_low if k < 8 else h_op)[:, 0, k, :]
                    act.activation(dst, side_bank(e)[:, 0:NT], ACT.Copy).then_inc(op_hi, 1)
                elif what == "turn":
                    c, t = e[1:]
                    wait_full(act, *e)
                    h0 = HEADS if CHUNKS[c][1] == "k" else 4 * NTH[c]
                    freed(act.activation(qk_t[:, h0:h0 + 4, t * P:(t + 1) * P],
                                         side_bank(e)[:, :].rearrange("p (h n) -> p h n", h=4), ACT.Copy), e)
                elif what == "turn_p":
                    n = P if units[e[1]][1] == 0 else NT
                    wait_full(act, *e)
                    freed(act.activation(probs_t[:, 0:n], side_bank(e)[:, 0:n], ACT.Copy), e)
                elif what == "scores":
                    u = e[1]
                    n = P if units[u][1] == 0 else NT
                    act.wait_ge(neg_max_ready, u + 1)
                    freed(act.activation(probs[:, 0:n], side_bank(e)[:, 0:n], ACT.Exp, bias=neg_max[:, u:u + 1],
                                         scale=SCALE, accum_out=row_sum[:, u:u + 1]), e)
                elif what == "denominator":
                    g = e[1]
                    act.wait_ge(sink_shifted, g + 1)
                    act.activation(sink_exp[:, 12 * g:12 * g + 12], inv_sum[:, 12 * g:12 * g + 12], ACT.Exp)\
                        .then_inc(sink_exped, 1)
                elif what == "evac":
                    c, t = e[1:]
                    kind = CHUNKS[c][1]
                    src = acc(c, t)[:, :]
                    if kind in GATED:
                        wait_chunk(act, c)
                        n = nth_gate[c, t]
                        if n >= 2:
                            wait_acc(act, *gate_chunks[n - 2])
                        if n == 0:
                            act.wait_ge(roped_ready, len(nth_roped))
                        if CHUNKS[c][0] == 1 and CHUNKS[gate_chunks[n - 1][0]][0] == 0:
                            wait_free(act, "h", 1, KT - 1)
                        act.activation(silu[:, n % 2, :], src, ACT.Silu).then_inc(silu_ready, 1)
                    elif kind in ("v", "ub", "uc"):
                        wait_chunk(act, c)
                        if kind == "ub" and t == 0:
                            wait_full(act, "pv", len(units) - 1)
                            act.wait_ge(v_stored, 16)
                        dst = u_pool[:, t, NTH[c] * CW:(NTH[c] + 1) * CW] if kind == "uc" else v_nat[:, t, :]
                        act.activation(dst, src, ACT.Copy).then_inc(acc_free[c % 2], 1)
                    elif kind == "vd":
                        n = TOKS * NTH[c] + t
                        act.wait_ge(ln_var_ready, n + 1)
                        act.activation(ln_std[:, :], ln_mv[:, :, 1], ACT.Sqrt).then_inc(ln_root, 1)
                elif what in ("dft_ctx", "dft_lat"):
                    wait_full(act, *e)
                    dst, n = (dft_c, 256) if what == "dft_ctx" else (dft_l, CW)
                    freed(act.activation(dst[:, :], side_bank(e)[:, 0:n], ACT.Copy), e)
                elif what == "pool":
                    g, j = e[1:]
                    wait_full(act, *e)
                    freed(act.activation(pooled[:, 2 * g + j, :], side_bank(e)[:, 0:NT], ACT.Copy), e)
                elif what == "mix":
                    c, t = e[1:]
                    wait_full(act, *e)
                    for i in range(2):
                        h = 2 * NTH[c] + i
                        last = act.activation(mixed[:, t, 1024 + h * GROUP:1024 + (h + 1) * GROUP],
                                              side_bank(e)[:, i * GROUP:(i + 1) * GROUP], ACT.Identity,
                                              bias=sgu_b_sb[:, h:h + 1], scale=1.0)
                    freed(last, e)
                elif what == "gate_y":
                    if e[2] == 0:
                        square_y(e[1])
                elif what == "residual":
                    residual_root(e[1])
                    if e[1] == 0:
                        norm_x(1)

            act.dma_start(cond_in[:, :, :], cond_cols).then_inc(cond_landed, 16)
            for t in range(TOKS):
                src = x_prompt[0] if t == 0 else x_sample[0, (t - 1) * P:t * P, :]
                act.dma_start(x[:, t, :], src).then_inc(x_in, 16)
            act.wait_ge(cond_landed, 16)
            act.wait_ge(cleared, 1)
            act.activation(cond[:, :, 0:2], cond_in[:, :, :], ACT.Silu).then_inc(cond_ready, 1)
            norm_x(0)
            for half in range(2):
                round_half(half)
            for p in places():
                for e in table.get(p, ()):
                    part(e)
                if p[0] == "at" and p[2] % 2 and 8 * p[1] + p[2] // 2 + 2 < 8 * len(CHUNKS):
                    round_half(8 * p[1] + p[2] // 2 + 2)

        @block.vector
        def _(dve):
            own = [0]

            def then_own(ins):
                own[0] += 1
                ins.then_inc(dve_own, 1)
                dve.wait_ge(dve_own, own[0])

            def split_half(half):
                dve.wait_ge(hi_ready, half + 1)
                n = nth_load["mm", half // 2]
                src = raw[:, n % RAW, (half % 2) * 2 * CW:(half % 2 + 1) * 2 * CW]
                hi = w_hi[:, half % WRING, :, :].rearrange("p k n -> p (k n)").bitcast(F32)
                dve.tensor_tensor(w_lo[:, half % WRING, :, :].rearrange("p k n -> p (k n)"), src, hi, ALU.subtract)\
                    .then_inc(lo_ready, 1)

            def finish_rows(m, dst):
                if m in SHIFT_BLOCK:
                    return
                dve.wait_ge(weight_in, 16 * (NORM_BLOCKS.index(m) + 1))
                dve.scalar_tensor_tensor(out=dst[:, :], in0=dst[:, :], scalar=1.0 if m in SCALE_BLOCK else 0.0,
                                         in1=weight_rows[:, :], op0=ALU.add, op1=ALU.mult).then_inc(rows_done, 1)

            def norm_x(layer):
                dve.wait_ge(x_squared, TOKS * (layer + 1))
                dve.tensor_scalar(stat[:, 5, :], stat[:, 4, :], 1.0 / D, EPS, ALU.mult, ALU.add).then_inc(x_mean, 1)
                dve.wait_ge(x_root, layer + 1)
                then_own(dve.reciprocal(stat[:, 7, :], stat[:, 6, :]))
                for t in range(TOKS):
                    dve.tensor_scalar(mixed[:, t, :], x[:, t, :], stat[:, 7, t:t + 1], None, ALU.mult)\
                        .then_inc(xn_ready, 1)

            def residual(layer):
                dve.wait_ge(y_squared, TOKS * N_OUT * (layer + 1))
                then_own(dve.tensor_reduce(stat[:, 0, :], sq[:, :, :], AX.X, ALU.add))
                dve.tensor_scalar(stat[:, 1, :], stat[:, 0, :], 1.0 / D, EPS, ALU.mult, ALU.add).then_inc(y_mean, 1)
                dve.wait_ge(y_root, layer + 1)
                then_own(dve.reciprocal(stat[:, 3, :], stat[:, 2, :]))
                wait_free(dve, "gate_y", layer * L1 + L1 - 1, 1)
                for t in range(TOKS):
                    dve.scalar_tensor_tensor(out=x[:, t, :], in0=mixed[:, t, :], scalar=stat[:, 3, t:t + 1],
                                             in1=x[:, t, :], op0=ALU.mult, op1=ALU.add).then_inc(x_ready, 1)

            def rotate(c, t):
                n = nth_roped[c, t]
                src = acc(c, t)
                if n:
                    prev = next(ct for ct, i in nth_roped.items() if i == n - 1)
                    wait_full(dve, "turn", *prev)
                if n == 1:
                    dve.wait_ge(k_stored, 16)
                    wait_free(dve, "h", 0, KT - 1)
                if t == 0:
                    dve.tensor_copy(roped[:, :], src[:, :]).then_inc(roped_ready, 1)
                    return
                dve.wait_ge(attn_in, 16 * 5)
                a = "p (h a b f) -> p h a b f"
                s4 = src[:, :].rearrange(a, h=4, a=2, b=2)
                tmp4 = rope_tmp.rearrange(a, h=4, a=2, b=2)
                sin = rope_sb[:, 1, t - 1, :].rearrange("p (a b f) -> p a b f", a=2, b=2)
                cos = rope_sb[:, 0, t - 1, :].unsqueeze(1).to_broadcast([P, 4, P])
                if n > 1:
                    dve.wait_ge(roped_ready, n)
                for b in range(2):
                    dve.tensor_tensor(tmp4[:, :, :, b, :], s4[:, :, :, 1 - b, :],
                                      sin[:, :, b, :].unsqueeze(1).to_broadcast([P, 4, 2, 32]), ALU.mult)
                then_own(dve.tensor_tensor(roped[:, :].rearrange("p (h d) -> p h d", h=4),
                                           src[:, :].rearrange("p (h d) -> p h d", h=4), cos, ALU.mult))
                dve.tensor_tensor(roped[:, :], roped[:, :], rope_tmp, ALU.add).then_inc(roped_ready, 1)

            def part(e):
                what = e[0]
                if what == "ada":
                    m, k, n = e[1:]
                    dst = gate if m in GATE_BLOCK else rows
                    wait_full(dve, *e)
                    if k == 0:
                        dve.wait_ge(bias_in, 16 * (m + 1))
                        wait_full(dve, *{2: ("cols", 1), 3: ("cols", 0), 4: ("cols", 3),
                                         5: ("gate_y", L1 - 1, 1)}[m])
                        freed(dve.tensor_tensor(dst[:, :], side_bank(e)[:, :], bias_rows[:, :], ALU.add), e)
                    else:
                        wait_free(dve, *ada_entry[m, k - 1])
                        freed(dve.tensor_tensor(dst[:, :], side_bank(e)[:, :], dst[:, :], ALU.add), e)
                    if k + n == KT:
                        wait_free(dve, *e)
                        finish_rows(m, dst)
                elif what == "h":
                    layer, k = e[1:]
                    j, i = divmod(k, 4)
                    if k == 0:
                        wait_free(dve, "cols", SCALE_BLOCK[layer])
                        wait_free(dve, "cols", SHIFT_BLOCK[layer])
                    elif k:
                        wait_free(dve, "h", layer, k - 1)
                    dve.wait_ge(op_hi, nth_op("h", layer, k) + 1)
                    for c_, lo_, hi_ in ((0, 0, P), (1, P, NT)):
                        col = 32 * j + c_
                        last = dve.tensor_scalar(h_tmp[:, lo_:hi_], side_bank(e)[:, lo_:hi_],
                                                 scale_t[:, i, col:col + 1], shift_t[:, i, col:col + 1],
                                                 ALU.mult, ALU.add)
                    then_own(last)
                    freed(dve.tensor_tensor(h_op[:, 1, k, :], h_tmp, h_op[:, 0, k, :].bitcast(F32), ALU.subtract), e)
                elif what == "o":
                    layer, k = e[1:]
                    dst = o_low if k < 8 else h_op
                    dve.wait_ge(op_hi, nth_op("o", layer, k) + 1)
                    freed(dve.tensor_tensor(dst[:, 1, k, :], side_bank(e)[:, 0:NT], dst[:, 0, k, :].bitcast(F32),
                                            ALU.subtract), e)
                elif what == "scores":
                    u = e[1]
                    t = units[u][1]
                    n = P if t == 0 else NT
                    s = side_bank(e)
                    wait_full(dve, *e)
                    if u == 0:
                        dve.wait_ge(attn_in, 16 * 5)
                        then_own(dve.tensor_scalar(neg_sinks[:, :], sinks[:, :], -1.0, None, ALU.mult))
                    if t:
                        other = slice((2 - t) * P, (3 - t) * P)
                        then_own(dve.tensor_tensor(s[:, other], s[:, other], mask_sb[:, t - 1, :], ALU.add))
                    then_own(dve.tensor_reduce(row_max[:, u:u + 1], s[:, 0:n], AX.X, ALU.max))
                    dve.tensor_scalar(neg_max[:, u:u + 1], row_max[:, u:u + 1], -SCALE, neg_sinks[:, u:u + 1],
                                      ALU.mult, ALU.min).then_inc(neg_max_ready, 1)
                elif what == "pv":
                    g, t, i = units[e[1]]
                    h = 4 * g + i
                    wait_full(dve, *e)
                    freed(dve.tensor_copy(mixed[:, t, h * HD:(h + 1) * HD], side_bank(e)[:, 0:HD]), e)
                elif what == "denominator":
                    g = e[1]
                    s = slice(12 * g, 12 * g + 12)
                    dve.wait_ge(neg_max_ready, 12 * (g + 1))
                    dve.tensor_tensor(inv_sum[:, s], sinks[:, s], neg_max[:, s], ALU.add).then_inc(sink_shifted, 1)
                    dve.wait_ge(sink_exped, g + 1)
                    then_own(dve.tensor_tensor(sink_exp[:, s], sink_exp[:, s], row_sum[:, s], ALU.add))
                    dve.reciprocal(inv_sum[:, s], sink_exp[:, s]).then_inc(inv_ready, 1)
                elif what == "evac":
                    c, t = e[1:]
                    kind = CHUNKS[c][1]
                    src = acc(c, t)
                    if kind in ROPED:
                        wait_chunk(dve, c)
                        rotate(c, t)
                    elif kind in GATED:
                        n = nth_gate[c, t]
                        dve.wait_ge(silu_ready, n + 1)
                        g_sb = silu[:, n % 2, :]
                        col = GATED[kind] + CW * NTH[c]
                        if kind == "ga":
                            g = NTH[c]
                            dve.wait_ge(inv_ready, g + 1)
                            if t == 0:
                                wait_free(dve, "pv", 12 * g + 11)
                            for i in range(4):
                                u = 12 * g + 4 * t + i
                                o = mixed[:, t, col + i * HD:col + (i + 1) * HD]
                                last = dve.scalar_tensor_tensor(out=o, in0=o, scalar=inv_sum[:, u:u + 1],
                                                                in1=g_sb[:, i * HD:(i + 1) * HD],
                                                                op0=ALU.mult, op1=ALU.mult)
                            last.then_inc(acc_free[c % 2], 1)
                        else:
                            if kind == "gb" and t == 0:
                                wait_free(dve, "dft_ch", 3)
                            if kind == "gc" and t == 0:
                                for g in (2 * NTH[c], 2 * NTH[c] + 1):
                                    for part_ in range(2):
                                        wait_free(dve, "pool_mix", g, part_)
                            if kind == "gd":
                                wait_acc(dve, c - 2, t)
                            o = mixed[:, t, col:col + CW]
                            dve.tensor_tensor(o, o, g_sb, ALU.mult).then_inc(acc_free[c % 2], 1)
                    elif kind == "vd":
                        n = TOKS * NTH[c] + t
                        wait_chunk(dve, c)
                        if n:
                            dve.wait_ge(vn_ready, n)
                        for i in range(2):
                            last = dve.bn_stats(ln_stats[:, i, :], src[:, i * GROUP:(i + 1) * GROUP])
                        then_own(last)
                        for i in range(2):
                            last = dve.bn_aggr(ln_mv[:, i, :], ln_stats[:, i, :])
                        then_own(last)
                        dve.tensor_scalar(ln_mv[:, :, 1], ln_mv[:, :, 1], EPS, None, ALU.add).then_inc(ln_var_ready, 1)
                    elif kind == "ud":
                        wait_chunk(dve, c)
                        wait_free(dve, "mix", vd_chunks[NTH[c]], t)
                        o = mixed[:, t, 1024 + CW * NTH[c]:1024 + CW * (NTH[c] + 1)]
                        dve.tensor_tensor(o, o, src[:, :], ALU.mult).then_inc(acc_free[c % 2], 1)
                elif what == "evac2":
                    c, t = e[1:]
                    n = TOKS * NTH[c] + t
                    src = acc(c, t)
                    dve.wait_ge(ln_root, n + 1)
                    then_own(dve.reciprocal(ln_std[:, :], ln_std[:, :]))
                    dve.wait_ge(sgu_in, 16)
                    if NTH[c]:
                        wait_full(dve, "mix", vd_chunks[0], t)
                    col = CW * NTH[c]
                    for i in range(2):
                        o = v_normed[:, t, i * GROUP:(i + 1) * GROUP]
                        last = dve.scalar_tensor_tensor(
                            out=o, in0=src[:, i * GROUP:(i + 1) * GROUP], scalar=ln_mv[:, i, 0:1],
                            in1=sgu_n[:, col + i * GROUP:col + (i + 1) * GROUP], op0=ALU.subtract, op1=ALU.mult)
                    last.then_inc(acc_free[c % 2], 1)
                    wait_acc(dve, c, t)
                    for i in range(2):
                        o = v_normed[:, t, i * GROUP:(i + 1) * GROUP]
                        last = dve.tensor_scalar(o, o, ln_std[:, i:i + 1], None, ALU.mult)
                    last.then_inc(vn_ready, 1)
                elif what == "dft_ch":
                    g = e[1]
                    wait_full(dve, *e)
                    freed(dve.tensor_copy(mixed[:, :, ATT + g * P:ATT + (g + 1) * P],
                                          side_bank(e)[:, 0:NT].rearrange("p (t n) -> p t n", t=TOKS)), e)
                elif what == "pool_mix":
                    g, part_ = e[1:]
                    wait_full(dve, *e)
                    toks = (0, 1) if part_ == 0 else (2,)
                    for i, t in enumerate(toks):
                        last = dve.tensor_tensor(mixed[:, t, g * GROUP:(g + 1) * GROUP],
                                                 side_bank(e)[:, i * GROUP:(i + 1) * GROUP],
                                                 pool_s[:, g * GROUP:(g + 1) * GROUP], ALU.mult)
                    freed(last, e)
                elif what == "gate_y":
                    c, n_cond = e[1:]
                    col = CHUNKS[c][2]
                    wait_full(dve, *e)
                    wait_acc(dve, c, 0 if n_cond == 0 else TOKS - 1)
                    for t in (0,) if n_cond == 0 else (1, 2):
                        y = mixed[:, t, col:col + CW]
                        last = dve.tensor_tensor(y, y, side_bank(e)[:, :], ALU.mult)
                    freed(last, e)
                elif what == "residual":
                    residual(e[1])
                    if e[1] == 0:
                        norm_x(1)

            norm_x(0)
            for m, dst in ((0, rows), (1, gate)):
                dve.wait_ge(ada_done, KT * (m + 1))
                dve.wait_ge(bias_in, 16 * (m + 1))
                dve.tensor_tensor(dst[:, :], bank[3 + m][:, :], bias_rows[:, :], ALU.add).then_inc(bias_used, 1)
                dve.wait_ge(bias_used, m + 1)
                finish_rows(m, dst)
            for half in range(2):
                split_half(half)
            for p in places():
                for e in table.get(p, ()):
                    part(e)
                if p[0] == "at" and p[2] % 2 and 8 * p[1] + p[2] // 2 + 2 < 8 * len(CHUNKS):
                    split_half(8 * p[1] + p[2] // 2 + 2)


def shape_constants():
    import numpy as np
    identity = np.eye(P, dtype=np.float32)
    row_select = np.zeros((P, 2, P), np.float32)
    for j in range(4):
        for cond in range(2):
            row_select[32 * j + cond, cond, :] = 1.0
    n_freq = HD // 4
    inv = (np.float32(10000.0) ** (-np.arange(n_freq, dtype=np.float32) / np.float32(n_freq))).astype(np.float32)
    pos = np.arange(2 * P)
    angle = np.stack([(pos // 64)[:, None].astype(np.float32) * inv,
                      (pos % 64)[:, None].astype(np.float32) * inv], axis=1)
    cos = np.repeat(np.cos(angle)[:, :, None, :], 2, axis=2)
    sin = np.stack([-np.sin(angle), np.sin(angle)], axis=2)
    rope = np.stack([cos.reshape(2, P, HD), sin.reshape(2, P, HD)]).transpose(2, 0, 1, 3)
    i, j = np.arange(P)[:, None], np.arange(P)[None, :]
    mask = np.stack([np.where(j <= i, 0.0, -1e30), np.where(i <= j, 0.0, -1e30)], axis=1)

    def cos_sin(n):
        a = 2 * np.pi * (np.outer(np.arange(n), np.arange(n)) % n) / n
        return np.cos(a) / np.sqrt(n), np.sin(a) / np.sqrt(n)

    c128, s128 = cos_sin(P)
    c256, s256 = cos_sin(2 * P)
    both = np.concatenate([c256, s256], axis=1).reshape(2, P, 4 * P).transpose(1, 0, 2).reshape(P, 8 * P)
    dft = np.concatenate([c128, s128, both, c128, -s128], axis=1)

    def pool(length, window):
        at = np.arange(length)
        lo, hi = np.clip(at - window // 2, 0, length), np.clip(at + window // 2, 0, length)
        src = np.arange(length)[:, None]
        return ((src >= lo) & (src < hi)) / (hi - lo) - (src == at)

    ctx = np.stack([pool(P, w) for w in WINDOWS], axis=1)
    lat = np.stack([pool(2 * P, w) for w in WINDOWS], axis=1)
    own = np.stack([lat[:P, :, :P], lat[P:, :, P:]], axis=1)
    cross = np.stack([lat[:P, :, P:P + 8], lat[P:, :, P - 8:P]], axis=1)
    pool_mats = np.concatenate([ctx.reshape(P, -1), own.reshape(P, -1), cross.reshape(P, -1)], axis=1)
    return {name: np.ascontiguousarray(a, dtype=np.float32) for name, a in {
        "identity": identity, "row_select": row_select, "rope": rope, "window_mask": mask,
        "dft": dft, "pool_mats": pool_mats}.items()}


def kernel(x_prompt, x_sample, cache_k, cache_v, c, c_ctx, w_ada, b_ada, norm_pre, norm_post, w_in, w_out,
           attn_sink, pool_w, pool_scale, sgu_norm, sgu_w, sgu_b):
    import numpy as np
    import concourse.bacc as bacc
    from concourse.bass_utils import run_bass_kernel_spmd

    def spread(row):
        out = np.zeros((P, CW), np.float32)
        for j in range(4):
            for cond in range(2):
                out[32 * j + cond] = row[CW * j:CW * (j + 1)]
        return out

    a = {name: np.asarray(v) for name, v in dict(
        x_prompt=x_prompt, x_sample=x_sample, cache_k=cache_k, cache_v=cache_v, c=c, c_ctx=c_ctx, w_ada=w_ada,
        b_ada=b_ada, norm_pre=norm_pre, norm_post=norm_post, w_in=w_in, w_out=w_out, attn_sink=attn_sink,
        pool_w=pool_w, pool_scale=pool_scale, sgu_norm=sgu_norm, sgu_w=sgu_w, sgu_b=sgu_b).items()}
    norms = {SCALE_BLOCK: a["norm_pre"], GATE_BLOCK: a["norm_post"]}
    arrays = {
        "x_prompt": a["x_prompt"], "x_sample": a["x_sample"],
        "cond_cols": np.stack([a["c_ctx"], a["c"][0]]).reshape(2, KT, P).transpose(2, 1, 0),
        "w_ada": a["w_ada"],
        "ada_rows": np.stack([spread(a["b_ada"][layer, D * third:D * (third + 1)]) for layer, third in BLOCKS]),
        "norm_rows": np.stack([spread(next(v for ms, v in norms.items() if m in ms)[BLOCKS[m][0]])
                               for m in NORM_BLOCKS]),
        "w_in": a["w_in"], "w_out": a["w_out"],
        "cache_kt": a["cache_k"][0, 0].transpose(2, 1, 0),
        "cache_v": a["cache_v"][0, 0].reshape(P, CW),
        "sink_units": np.stack([a["attn_sink"][0, 4 * g + i] for g, _, i in head_units()]).reshape(1, 36),
        "pool_w": a["pool_w"], "pool_scale": a["pool_scale"], "sgu_norm": a["sgu_norm"],
        "sgu_wt": a["sgu_w"][0].transpose(2, 0, 1), "sgu_bt": a["sgu_b"][0].transpose(1, 0),
        **shape_constants(),
    }
    outs = {"y_prompt": (1, P, D), "y_sample": (1, 2 * P, D), "new_k": (P, CW), "new_v": (P, CW)}
    nc = bacc.Bacc("TRN2", target_bir_lowering=False, num_devices=1)
    feed, aps = {}, {}
    for name, v in arrays.items():
        v = np.ascontiguousarray(v)
        feed[f"in_{name}"] = v
        aps[name] = nc.dram_tensor(f"in_{name}", v.shape, mybir.dt.from_np(v.dtype), kind="ExternalInput").ap()
    for name, shape in outs.items():
        aps[name] = nc.dram_tensor(f"out_{name}", shape, F32, kind="ExternalOutput").ap()
    hybrid_step(nc, **aps)
    got = run_bass_kernel_spmd(nc, [feed], core_ids=[0]).results[0]
    cache_shape = (1, 1, P, KV_HEADS, HD)
    return (got["out_y_prompt"], got["out_y_sample"], got["out_new_k"].reshape(cache_shape),
            got["out_new_v"].reshape(cache_shape))
```

```python
from contextlib import ExitStack

import concourse.bass as bass
from concourse import mybir

F32 = mybir.dt.float32
F32R = mybir.dt.float32r
ALU = mybir.AluOpType
ACT = mybir.ActivationFunctionType
AX = mybir.AxisListType

P = 128
D = 2048
TOKS = 3
NT = TOKS * P
KT = D // P
CW = 512
PIECES = 4
PIECE = D // PIECES
HEADS, KV_HEADS, HD = 12, 4, 128
Q_PER_KV = HEADS // KV_HEADS
ATT = HEADS * HD
EPS = 1e-6
SCALE = HD ** -0.5
WINDOWS = (2, 4, 8, 16)
GROUP = 256

IN_CHUNKS = [
    [("v", 2048), ("k", 1536), ("q", 0), ("q", 512), ("q", 1024),
     ("ga", 2560), ("ga", 3072), ("ga", 3584), ("ub", 4096), ("gb", 4608)],
    [("uc", 0), ("uc", 512), ("vd", 3072), ("vd", 3584), ("gc", 1024), ("gc", 1536),
     ("ud", 2048), ("ud", 2560), ("gd", 4096), ("gd", 4608)],
]
N_IN = len(IN_CHUNKS[0])
N_OUT = D // CW
PER_LAYER = N_IN + N_OUT
CHUNKS = [(layer, kind, col) for layer in range(2)
          for kind, col in IN_CHUNKS[layer] + [("out", CW * j) for j in range(N_OUT)]]
NTH = [sum(x[:2] == CHUNKS[c][:2] for x in CHUNKS[:c]) for c in range(len(CHUNKS))]
ROPED = {"k": 0, "q": 1}
GATED = {"ga": 0, "gb": ATT, "gc": 0, "gd": 1024}
L1 = PER_LAYER
SHIFT_COL, SCALE_COL, GATE_COL = 0, 1, 2
BLOCKS = [(0, GATE_COL), (1, SCALE_COL), (1, SHIFT_COL), (1, GATE_COL)]
GATE_BLOCK = (0, 3)
SCALE_BLOCK, SHIFT_BLOCK = 1, 2
NORM_BLOCKS = [0, 1, 3]
SEAM_ADA = 5
WRING = 3
RAW = 3
QUARTERS = [(c, q) for q in range(4) for c in (0, 1)]
QUARTERS += [(c, q) for c in range(2, len(CHUNKS)) for q in range(4)]
NTH_QUARTER = {cq: n for n, cq in enumerate(QUARTERS)}


def head_units():
    return [(g, t, h) for g in range(HEADS // 4) for t in range(TOKS) for h in range(4)]


def timetable():
    at = {}

    def put(c, s, *entry):
        c, s = c + s // KT, s % KT
        at.setdefault(("at", c, s), []).append(entry)

    def pre(c, *entry):
        at.setdefault(("pre", c), []).append(entry)

    for b in range(4):
        n = 0
        for w in range(2):
            for i in range(4):
                if b == 0:
                    pre(0, "first_ada", b, w, i)
                    if n == 5:
                        pre(0, "norm", 0)
                        pre(0, "first_weights")
                else:
                    put(n // 4, 4 * (b - 1) + (n % 4) * 3 // 4, "first_ada", b, w, i)
                n += 1
        for k in range(4 * b, 4 * b + 2):
            if k == 4 * b:
                for w in range(2):
                    (pre(0, "first_cols", b, w) if b == 0 else put(1, 4 * b - 2, "first_cols", b, w))
            (pre(0, "h", 0, k) if b == 0 else put(1, 4 * b - 1, "h", 0, k))
        for k in range(4 * b + 2, 4 * b + 4):
            put(0, k - 2, "h", 0, k)
    pre(L1, "cols", SHIFT_BLOCK)
    for t in range(TOKS):
        pre(L1, "evac", L1 - 1, t)
    pre(L1, "residual", 0)
    pre(L1, "ada", GATE_BLOCK[1], 0, SEAM_ADA)
    pre(L1, "xn", 1, 0)
    for k in range(3):
        pre(L1, "h", 1, k)
    pre(L1, "xn", 1, 1)
    for k in range(3, KT):
        put(L1, k - 3, "h", 1, k)
        if k % 4 == 1 and k < 12:
            put(L1, k - 3, "xn", 1, k // 4 + 1)
    for c, (layer, kind, _) in enumerate(CHUNKS):
        nxt = c + 1
        if kind == "out":
            for n in range(2):
                put(c, 10 + 2 * n, "gate_y", c, n)
            if c not in (L1 - 1, 2 * L1 - 1):
                for t in range(TOKS):
                    put(nxt, t, "evac", c, t)
            continue
        step = {"k": 3, "q": 3, "vd": 2}.get(kind, 1)
        if c == 0:
            for t in range(TOKS):
                put(1, 12 + t, "evac", c, t)
            continue
        for t in range(TOKS):
            put(nxt, step * t, "evac", c, t)
            if kind in ROPED:
                put(nxt, step * t + 2, "turn", c, t)
            if kind == "vd":
                put(nxt, step * t + 1, "evac2", c, t)
                put(nxt, step * t + 5, "mix", c, t)
    first = 3 * KT + 4
    for u in range(HEADS * TOKS):
        put(0, first + 2 * u + 2, "turn_p", u)
        put(0, first + 2 * u + 3, "pv", u)
    for u in range(HEADS * TOKS):
        put(0, first + 2 * u, "scores", u)
    for g in range(HEADS // 4):
        put(0, first + 2 * (12 * g + 11) + 4, "denominator", g)
    for k in range(8):
        put(8, k, "o", 0, k)
        put(L1 + 5 + k // 4, 6 + k % 4, "o", 1, k)
        for layer in range(2):
            put(layer * L1 + N_IN, k + 1, "o", layer, 8 + k)
    for g in range(4):
        put(9, 3 + 3 * g, "dft_ctx", g)
        put(9, 4 + 3 * g, "dft_lat", g)
        put(9, 5 + 3 * g, "dft_ch", g)
        c, s = L1 + 1 + g // 2, 4 + 4 * (g % 2)
        for j in range(2):
            put(c, s + j, "pool", g, j)
            put(c, s + 2 + j, "pool_mix", g, j)
    rows = [(m, k) for m in range(3) for k in range(KT)]
    for n, (m, k) in enumerate(rows):
        put(2 + n // 4, 4 * (n % 4) + 3, "ada", m, k, 1)
    for n, k in enumerate(range(SEAM_ADA, KT)):
        put(L1 + n // 4, 4 * (n % 4) + 3, "ada", GATE_BLOCK[1], k, 1)
    put(10, 1, "cols", SCALE_BLOCK)
    end = len(CHUNKS)
    for t in range(TOKS):
        pre(end, "evac", end - 1, t)
    pre(end, "residual", 1)
    return at


SIDE = {"first_ada", "first_cols", "cols", "h", "gate_y", "ada", "turn", "turn_p", "pv", "scores", "o", "dft_ctx", "dft_lat",
        "dft_ch", "pool", "pool_mix", "mix"}


def places():
    for n, (c, q) in enumerate(QUARTERS):
        if q == 0:
            yield ("pre", c)
        for s in range(4 * q, 4 * q + 4):
            yield ("at", c, s)
    yield ("pre", len(CHUNKS))


def hybrid_step(nc, x_prompt, x_sample, cond_cols, w_ada, first_cols, ada_rows, norm_rows, w_in, w_out, cache_kt,
                cache_v, sink_units, pool_w, pool_scale, sgu_norm, sgu_wt, sgu_bt,
                identity, row_select, minus_lo_rows, rope, window_mask, dft, pool_mats,
                y_prompt, y_sample, new_k, new_v):
    table = timetable()
    side = [e for p in places() for e in table.get(p, ()) if e[0] in SIDE]
    nth_side = {e: n for n, e in enumerate(side)}
    assert len(nth_side) == len(side)

    loads = []
    for p in places():
        if p[0] == "at" and p[2] % 4 == 0 and NTH_QUARTER[p[1], p[2] // 4] + 1 < len(QUARTERS):
            loads.append(("mm", NTH_QUARTER[p[1], p[2] // 4] + 1))
        for e in table.get(p, ()):
            if e[0] == "first_ada":
                loads.append(e)
            if e[0] == "first_weights":
                loads.append(("mm", 0))
            if e[0] == "ada":
                loads += [("ada", e[1], e[2] + i) for i in range(e[3])]
    nth_first = {x: n for n, x in enumerate(x for x in loads if x[0] == "first_ada")}
    ring = [x for x in loads if x[0] != "first_ada"]
    nth_load = {x: n for n, x in enumerate(ring)}
    ada_entry = {(e[1], e[2] + i): e for e in side if e[0] == "ada" for i in range(e[3])}
    early = [("ada", e[1], e[2] + i) for e in side if e[0] == "ada" for i in range(e[3] - 1)]

    with ExitStack() as ctx:
        place = [(nc.sbuf_base + 63) // 64 * 64]

        def tensor(name, shape, dt=F32, at=None):
            size = 4
            for n in shape:
                size *= n
            if at is None:
                at = place[0]
                place[0] += (size + 31) // 32 * 32
            return nc.alloc_sbuf_tensor_at(name, [P, *shape], dt, offset=at)

        x = tensor("x", [TOKS, D])
        mixed = tensor("mixed", [TOKS, D])
        h_op = tensor("h_op", [2, KT, NT], F32R)
        region = place[0]
        qk_t = tensor("qk_t", [16, NT])
        u_pool = tensor("u_pool", [TOKS, 1024], at=region)
        pooled = tensor("pooled", [8, NT], at=region + 4 * TOKS * 1024)
        o_low = tensor("o_low", [2, 8, NT], F32R, at=region)
        raw_first = tensor("raw_first", [RAW, D], at=region)
        raw = tensor("raw", [RAW, D])
        w_hi = tensor("w_hi", [WRING, 2, CW], F32R)
        w_lo = tensor("w_lo", [WRING, 2, CW], F32R)
        ident = tensor("ident", [P])
        row_sel = tensor("row_sel", [2, P])
        row_sel_r = tensor("row_sel_r", [2, P], F32R)
        minus_lo = tensor("minus_lo", [1])
        cond = tensor("cond", [KT, 32])
        cond_in = tensor("cond_in", [KT, 2])
        scale_t = tensor("scale_t", [KT, 2])
        shift_t = tensor("shift_t", [KT, 2])
        first_c = tensor("first_c", [3, KT])
        col_sum = tensor("col_sum", [2, 4, 2])
        rows = tensor("rows", [CW])
        gate = tensor("gate", [CW])
        gate_parts = tensor("gate_parts", [CW], F32R)
        bias_rows = tensor("bias_rows", [CW])
        weight_rows = tensor("weight_rows", [CW])
        silu = tensor("silu", [2, CW])
        sinks = tensor("sinks", [36])
        neg_sinks = tensor("neg_sinks", [36])
        row_max = tensor("row_max", [36])
        neg_max = tensor("neg_max", [36])
        row_sum = tensor("row_sum", [36])
        sink_exp = tensor("sink_exp", [36])
        inv_sum = tensor("inv_sum", [36])
        sq = tensor("sq", [TOKS, 4])
        stat = tensor("stat", [8, TOKS])
        ln_stats = tensor("ln_stats", [2, 6])
        ln_mv = tensor("ln_mv", [2, 2])
        ln_std = tensor("ln_std", [2])
        area = place[0]

        def in_area(name, shape, at):
            return tensor(name, shape, at=area + 4 * at)

        v_nat = in_area("v_nat", [TOKS, CW], 0)
        cache_k_sb = in_area("cache_k_sb", [KV_HEADS, P], 1536)
        cache_v_sb = in_area("cache_v_sb", [CW], 2048)
        rope_sb = in_area("rope_sb", [2, 2, P], 2560)
        mask_sb = in_area("mask_sb", [2, P], 3072)
        probs = in_area("probs", [NT], 3328)
        probs_t = in_area("probs_t", [NT], 3712)
        dft_sb = in_area("dft_sb", [1536], 1536)
        dft_c = in_area("dft_c", [256], 3328)
        dft_l = in_area("dft_l", [CW], 3584)
        roped = in_area("roped", [CW], 4168)
        junk = in_area("junk", [CW], 4168)
        pool_m = in_area("pool_m", [1600], 0)
        pool_s = in_area("pool_s", [1024], 1600)
        pool_w_sb = in_area("pool_w_sb", [2, 2, GROUP], 2624)
        sgu_w_sb = in_area("sgu_w_sb", [4, P], 3648)
        sgu_b_sb = in_area("sgu_b_sb", [4], 4160)
        v_normed = in_area("v_normed", [TOKS, CW], 0)
        sgu_n = in_area("sgu_n", [1024], 1536)
        assert area + 4 * 4680 <= nc.sbuf_usable_end, (area + 4 * 4680, nc.sbuf_usable_end)
        rope_tmp = silu[:, 0, :]
        h_tmp = silu[:, 0, 0:NT]
        dft_128 = dft_sb[:, 0:256]
        dft_256 = dft_sb[:, 256:1280].rearrange("p (a n) -> p a n", a=2)
        dft_chan = dft_sb[:, 1280:1536]
        pool_ctx = pool_m[:, 0:512].rearrange("p (g n) -> p g n", g=4)
        pool_own = pool_m[:, 512:1536].rearrange("p (a g n) -> p a g n", a=2, g=4)
        pool_cross = pool_m[:, 1536:1600].rearrange("p (a g n) -> p a g n", a=2, g=4)

        bank = [ctx.enter_context(nc.psum_tensor(f"bank{i}", [P, CW], F32)) for i in range(8)]

        def acc(c, t):
            return bank[3 * (c % 2) + t]

        def sem(name):
            return ctx.enter_context(nc.semaphore(name))

        raw_in = [sem(f"raw_in{i}") for i in range(RAW)]
        first_raw_in = [sem(f"first_raw_in{i}") for i in range(RAW)]
        const_in = sem("const_in")
        cond_landed = sem("cond_landed")
        x_in = sem("x_in")
        attn_in = sem("attn_in")
        first_in = sem("first_in")
        bias_in = sem("bias_in")
        weight_in = sem("weight_in")
        dft_in = sem("dft_in")
        pool_in = sem("pool_in")
        pool_w_in = [sem("pool_w_in0"), sem("pool_w_in1")]
        sgu_in = sem("sgu_in")
        stored = sem("stored")
        k_stored = sem("k_stored")
        v_stored = sem("v_stored")
        cleared = sem("cleared")
        cond_ready = sem("cond_ready")
        ada_done = sem("ada_done")
        first_ready = sem("first_ready")
        hi_ready = sem("hi_ready")
        lo_ready = sem("lo_ready")
        mm_done = sem("mm_done")
        acc_free = [sem("acc_free0"), sem("acc_free1")]
        side_full = [sem("side_full0"), sem("side_full1")]
        side_free = [sem("side_free0"), sem("side_free1")]
        rows_done = sem("rows_done")
        op_hi = sem("op_hi")
        roped_ready = sem("roped_ready")
        neg_max_ready = sem("neg_max_ready")
        sink_shifted = sem("sink_shifted")
        sink_exped = sem("sink_exped")
        inv_ready = sem("inv_ready")
        silu_ready = sem("silu_ready")
        y_squared = sem("y_squared")
        y_mean = sem("y_mean")
        y_root = sem("y_root")
        x_ready = sem("x_ready")
        x_squared = sem("x_squared")
        x_mean = sem("x_mean")
        x_root = sem("x_root")
        x_scale = sem("x_scale")
        rows_selectable = sem("rows_selectable")
        xn_ready = sem("xn_ready")
        xn_act = sem("xn_act")
        ln_var_ready = sem("ln_var_ready")
        ln_root = sem("ln_root")
        vn_ready = sem("vn_ready")
        act_own = sem("act_own")
        dve_own = sem("dve_own")

        def side_bank(e):
            return bank[6 + nth_side[e] % 2]

        def wait_full(eng, *e):
            eng.wait_ge(side_full[nth_side[e] % 2], nth_side[e] // 2 + 1)

        def wait_free(eng, *e):
            eng.wait_ge(side_free[nth_side[e] % 2], nth_side[e] // 2 + 1)

        def filled(ins, e):
            ins.then_inc(side_full[nth_side[e] % 2], 1)

        def freed(ins, e):
            ins.then_inc(side_free[nth_side[e] % 2], 1)

        def wait_acc(eng, c, t):
            if CHUNKS[c][1] in ROPED:
                eng.wait_ge(roped_ready, nth_roped[c, t] + 1)
            else:
                before = sum(CHUNKS[b][1] not in ROPED for b in range(c % 2, c, 2))
                eng.wait_ge(acc_free[c % 2], TOKS * before + t + 1)

        def wait_chunk(eng, c):
            eng.wait_ge(mm_done, 2 * NTH_QUARTER[c, 3] + 2)

        def wait_load(eng, *what):
            n = nth_load[what]
            eng.wait_ge(raw_in[n % RAW], 16 * (n // RAW + 1))

        def half_ahead(p):
            if p[0] == "at" and p[2] % 2:
                half = 2 * NTH_QUARTER[p[1], p[2] // 4] + p[2] % 4 // 2 + 2
                return half if half < 2 * len(QUARTERS) else None

        def nth_op(kind, layer, k):
            return 2 * KT * layer + (KT if kind == "o" else 0) + k

        units = head_units()
        gate_chunks = [(c, t) for c in range(len(CHUNKS)) if CHUNKS[c][1] in GATED for t in range(TOKS)]
        nth_gate = {ct: n for n, ct in enumerate(gate_chunks)}
        roped_chunks = [c for c in range(len(CHUNKS)) if CHUNKS[c][1] in ROPED]
        nth_roped = {(c, t): TOKS * n + t for n, c in enumerate(roped_chunks) for t in range(TOKS)}
        out_chunks = [c for c in range(len(CHUNKS)) if CHUNKS[c][1] == "out"]
        nth_out = {c: n for n, c in enumerate(out_chunks)}
        first_q = roped_chunks[1]
        v_chunk = next(c for c in range(len(CHUNKS)) if CHUNKS[c][1] == "v")
        ub_chunk = next(c for c in range(len(CHUNKS)) if CHUNKS[c][1] == "ub")
        uc_chunks = [c for c in range(len(CHUNKS)) if CHUNKS[c][1] == "uc"]
        vd_chunks = [c for c in range(len(CHUNKS)) if CHUNKS[c][1] == "vd"]

        def gate_of(layer, k):
            kinds = (("ga", "gb"), ("gc", "gd"))[layer]
            col = k * P
            for c, (at_layer, kind, _) in enumerate(CHUNKS):
                if at_layer == layer and kind in kinds and GATED[kind] + CW * NTH[c] == col // CW * CW:
                    return c

        block = ctx.enter_context(nc.Block())

        @block.sync
        def _(sp):
            for what in loads:
                if what[0] == "first_ada":
                    n = nth_first[what]
                    if n >= RAW:
                        wait_full(sp, *list(nth_first)[n - RAW])
                    b, w, i = what[1:]
                    col = (SCALE_COL, SHIFT_COL)[w] * D + b * CW
                    sp.dma_start(raw_first[:, n % RAW, :].rearrange("p (k n) -> p k n", n=CW),
                                 w_ada[0].rearrange("(k p) n -> p k n", p=P)[:, 4 * i:4 * i + 4, col:col + CW])\
                        .then_inc(first_raw_in[n % RAW], 16)
                    continue
                n = nth_load[what]
                if n >= RAW:
                    old = ring[n - RAW]
                    if old[0] == "mm":
                        sp.wait_ge(lo_ready, 2 * old[1] + 2)
                    elif old in early:
                        sp.wait_ge(ada_done, early.index(old) + 1)
                    else:
                        wait_full(sp, *ada_entry[old[1:]])
                slot = raw[:, n % RAW, :]
                if what[0] == "ada":
                    layer, third = BLOCKS[what[1]]
                    src = w_ada[layer, what[2] * P:(what[2] + 1) * P, third * D:(third + 1) * D]
                    sp.dma_start(slot, src).then_inc(raw_in[n % RAW], 16)
                else:
                    c, quarter = QUARTERS[what[1]]
                    layer, kind, col = CHUNKS[c]
                    w = (w_out if kind == "out" else w_in)[layer].rearrange("(k p) n -> p k n", p=P)
                    sp.dma_start(slot.rearrange("p (k n) -> p k n", n=CW),
                                 w[:, 4 * quarter:4 * quarter + 4, col:col + CW])\
                        .then_inc(raw_in[n % RAW], 16)
            for t in range(TOKS):
                dst = y_prompt[0] if t == 0 else y_sample[0, (t - 1) * P:t * P, :]
                for j in range(PIECES):
                    sp.wait_ge(x_ready, PIECES * (TOKS + t) + j + 1)
                    cols = slice(j * PIECE, (j + 1) * PIECE)
                    sp.dma_start(dst[:, cols], x[:, t, cols]).then_inc(stored, 16)
            sp.wait_ge(stored, 16 * TOKS * PIECES)
            sp.wait_ge(k_stored, 16)
            sp.wait_ge(v_stored, 16)

        @block.gpsimd
        def _(pool):
            pool.memset(cond[:, :, :], 0.0).then_inc(cleared, 1)

            def load_bias(m):
                if m:
                    wait_free(pool, *ada_entry[m - 1, 0])
                pool.dma_start(bias_rows[:, :], ada_rows[m]).then_inc(bias_in, 16)

            def load_weight(n):
                if n:
                    pool.wait_ge(rows_done, n)
                pool.dma_start(weight_rows[:, :], norm_rows[n]).then_inc(weight_in, 16)

            def load_pool_w(g):
                if g >= 2:
                    wait_full(pool, "pool_mix", g - 2, 1)
                pool.dma_start(pool_w_sb[:, g % 2, :, :],
                               pool_w[0, g].rearrange("(a p) n -> p a n", p=P))\
                    .then_inc(pool_w_in[g % 2], 16)

            pool.dma_start(ident[:, :], identity).then_inc(const_in, 16)
            pool.dma_start(first_c[:, :, :], first_cols).then_inc(first_in, 16)
            pool.dma_start(row_sel[:, :, :], row_select).then_inc(const_in, 16)
            pool.dma_start(minus_lo[:, :], minus_lo_rows).then_inc(const_in, 16)
            wait_full(pool, "first_ada", 3, 1, 3)
            pool.dma_start(rope_sb[:, :, :, :], rope).then_inc(attn_in, 16)
            pool.dma_start(mask_sb[:, :, :], window_mask).then_inc(attn_in, 16)
            pool.dma_start(cache_k_sb[:, :, :], cache_kt).then_inc(attn_in, 16)
            pool.dma_start(cache_v_sb[:, :], cache_v).then_inc(attn_in, 16)
            pool.dma_start(sinks[:, :], sink_units.partition_broadcast(P)).then_inc(attn_in, 16)
            load_bias(0)
            load_weight(0)
            wait_acc(pool, v_chunk, 0)
            pool.dma_start(new_v, v_nat[:, 0, :]).then_inc(v_stored, 16)
            pool.wait_ge(roped_ready, 1)
            pool.dma_start(new_k, roped[:, :]).then_inc(k_stored, 16)
            load_bias(1)
            load_weight(1)
            load_bias(2)
            wait_full(pool, "pv", len(units) - 1)
            pool.dma_start(dft_sb[:, :], dft).then_inc(dft_in, 16)
            load_weight(2)
            load_bias(3)
            wait_full(pool, "dft_ch", 3)
            pool.dma_start(pool_m[:, :], pool_mats).then_inc(pool_in, 16)
            pool.dma_start(pool_s[:, :], pool_scale.partition_broadcast(P)).then_inc(pool_in, 16)
            pool.dma_start(sgu_w_sb[:, :, :], sgu_wt).then_inc(pool_in, 16)
            pool.dma_start(sgu_b_sb[:, :], sgu_bt).then_inc(pool_in, 16)
            for g in range(4):
                load_pool_w(g)
            wait_free(pool, "pool_mix", 3, 1)
            wait_free(pool, "pool_mix", 3, 0)
            pool.dma_start(sgu_n[:, :], sgu_norm.partition_broadcast(P)).then_inc(sgu_in, 16)

        @block.tensor
        def _(pe):
            def ada_products(dst, m, k, start, stop):
                n = nth_load[("ada", m, k)]
                wait_load(pe, "ada", m, k)
                for j in range(4):
                    last = pe.matmul(dst[32 * j:32 * j + 32, :], cond[:, k, :],
                                     raw[:, n % RAW, CW * j:CW * (j + 1)],
                                     start=start, stop=stop)
                return last

            def operand(layer, kind, part, k, t):
                src = o_low if kind == "out" and k < 8 else h_op
                return src[:, part, k, t * P:(t + 1) * P]

            def k_step(c, k):
                layer, kind, _ = CHUNKS[c]
                if k == 0 and c >= 2:
                    wait_acc(pe, c - 2, TOKS - 1)
                half = 2 * NTH_QUARTER[c, k // 4] + k % 4 // 2
                if k % 2 == 0:
                    pe.wait_ge(lo_ready, half + 1)
                if c in (0, 1, L1):
                    wait_free(pe, "h", layer, k)
                if c in (N_IN, L1 + N_IN):
                    wait_free(pe, "o", layer, k)
                hi = w_hi[:, half % WRING, k % 2, :]
                lo = w_lo[:, half % WRING, k % 2, :]
                for t in range(TOKS):
                    out = acc(c, t)[:, :]
                    pe.matmul(out, operand(layer, kind, 0, k, t), hi, start=k == 0, stop=False)
                    pe.matmul(out, operand(layer, kind, 0, k, t), lo, start=False, stop=False)
                    last = pe.matmul(out, operand(layer, kind, 1, k, t), hi, start=False, stop=k == KT - 1)
                if k % 2:
                    last.then_inc(mm_done, 1)

            def side_product(e):
                n = nth_side[e]
                out = side_bank(e)
                what = e[0]
                if n >= 2:
                    pe.wait_ge(side_free[n % 2], n // 2)
                if what == "first_ada":
                    i = e[3]
                    if e[1:] == (0, 0, 0):
                        pe.wait_ge(cond_ready, 2)
                    slot = nth_first[e] % RAW
                    pe.wait_ge(first_raw_in[slot], 16 * (nth_first[e] // RAW + 1))
                    for j in range(4):
                        last = pe.matmul(out[32 * j:32 * j + 32, :], cond[:, 4 * i + j, :],
                                         raw_first[:, slot, CW * j:CW * (j + 1)], start=True, stop=True)
                elif what == "first_cols":
                    b, w = e[1:]
                    wait_free(pe, "first_ada", b, w, 3)
                    pe.wait_ge(const_in, 48)
                    for i in range(4):
                        last = pe.transpose(out[:, i * P:(i + 1) * P], (rows, gate)[w][:, i * P:(i + 1) * P],
                                            ident[:, :])
                elif what == "ada":
                    m, k0, count = e[1:]
                    for k in range(k0, k0 + count):
                        last = ada_products(out, m, k, k == k0, k == k0 + count - 1)
                        if k < k0 + count - 1:
                            last.then_inc(ada_done, 1)
                elif what == "cols":
                    if e[1] == SCALE_BLOCK:
                        pe.wait_ge(rows_done, NORM_BLOCKS.index(e[1]) + 1)
                    else:
                        wait_free(pe, *ada_entry[e[1], KT - 1])
                    for i in range(4):
                        last = pe.transpose(out[:, i * P:(i + 1) * P], rows[:, i * P:(i + 1) * P], ident[:, :])
                elif what == "h":
                    layer, k = e[1:]
                    if k % 4 == 0:
                        pieces = PIECES * layer + k // 4 + 1
                        pe.wait_ge(xn_ready, (TOKS - 1) * pieces)
                        pe.wait_ge(xn_act, pieces)
                    for t in range(TOKS):
                        last = pe.transpose(out[:, t * P:(t + 1) * P], mixed[:, t, k * P:(k + 1) * P], ident[:, :])
                elif what == "o":
                    layer, k = e[1:]
                    wait_acc(pe, gate_of(layer, k), TOKS - 1)
                    for t in range(TOKS):
                        last = pe.transpose(out[:, t * P:(t + 1) * P], mixed[:, t, k * P:(k + 1) * P], ident[:, :])
                elif what == "gate_y":
                    c, n_cond = e[1:]
                    layer, _, col = CHUNKS[c]
                    j = col // CW
                    pe.wait_ge(rows_done, NORM_BLOCKS.index(GATE_BLOCK[layer]) + 1)
                    pe.wait_ge(rows_selectable, 1)
                    last = pe.matmul(out[:, :], row_sel_r[32 * j:32 * j + 32, n_cond, :],
                                     gate_parts[32 * j:32 * j + 32, :], start=True, stop=True)
                elif what == "turn":
                    c, t = e[1:]
                    pe.wait_ge(roped_ready, nth_roped[c, t] + 1)
                    for h in range(4):
                        last = pe.transpose(out[:, h * P:(h + 1) * P], roped[:, h * P:(h + 1) * P], ident[:, :])
                elif what == "scores":
                    g, t, i = units[e[1]]
                    h = 4 * g + i
                    kv = h // Q_PER_KV
                    wait_free(pe, "turn", first_q + g, t)
                    for s in range(1 if t == 0 else TOKS):
                        wait_free(pe, "turn", roped_chunks[0], s)
                    q = qk_t[:, h, t * P:(t + 1) * P]
                    if t == 0:
                        last = pe.matmul(out[:, 0:P], q, qk_t[:, HEADS + kv, 0:P], start=True, stop=True)
                    else:
                        pe.wait_ge(attn_in, 16 * 5)
                        pe.matmul(out[:, 0:2 * P], q, qk_t[:, HEADS + kv, P:NT], start=True, stop=True)
                        last = pe.matmul(out[:, 2 * P:NT], q, cache_k_sb[:, kv, :], start=True, stop=True)
                elif what == "turn_p":
                    u = e[1]
                    wait_free(pe, "scores", u)
                    for s in range(1 if units[u][1] == 0 else TOKS):
                        last = pe.transpose(out[:, s * P:(s + 1) * P], probs[:, s * P:(s + 1) * P], ident[:, :])
                elif what == "pv":
                    u = e[1]
                    g, t, i = units[u]
                    kv = (4 * g + i) // Q_PER_KV
                    wait_free(pe, "turn_p", u)
                    wait_acc(pe, v_chunk, TOKS - 1)
                    vs = slice(kv * HD, (kv + 1) * HD)
                    values = [v_nat[:, 0, vs]] if t == 0 else [v_nat[:, 1, vs], v_nat[:, 2, vs], cache_v_sb[:, vs]]
                    for s, v in enumerate(values):
                        last = pe.matmul(out[:, 0:HD], probs_t[:, s * P:(s + 1) * P], v,
                                         start=s == 0, stop=s == len(values) - 1)
                elif what == "dft_ctx":
                    ch = slice(e[1] * P, (e[1] + 1) * P)
                    wait_acc(pe, ub_chunk, 0)
                    pe.wait_ge(dft_in, 16)
                    last = pe.matmul(out[:, 0:256], v_nat[:, 0, ch], dft_128, start=True, stop=True)
                elif what == "dft_lat":
                    ch = slice(e[1] * P, (e[1] + 1) * P)
                    wait_acc(pe, ub_chunk, TOKS - 1)
                    for a in range(2):
                        last = pe.matmul(out[:, :], v_nat[:, 1 + a, ch], dft_256[:, a, :], start=a == 0, stop=a == 1)
                elif what == "dft_ch":
                    wait_free(pe, "dft_ctx", e[1])
                    wait_free(pe, "dft_lat", e[1])
                    pairs = [(dft_c[:, 0:P], dft_c[:, P:2 * P])]
                    pairs += [(dft_l[:, a * P:(a + 1) * P], dft_l[:, (2 + a) * P:(3 + a) * P]) for a in range(2)]
                    for t, (cos_part, sin_part) in enumerate(pairs):
                        o = out[:, t * P:(t + 1) * P]
                        pe.matmul(o, cos_part, dft_chan[:, 0:P], start=True, stop=False)
                        last = pe.matmul(o, sin_part, dft_chan[:, P:2 * P], start=False, stop=True)
                elif what == "pool":
                    g, j = e[1:]
                    ch = slice(g * GROUP + j * P, g * GROUP + (j + 1) * P)
                    wait_acc(pe, uc_chunks[g // 2], TOKS - 1)
                    pe.wait_ge(pool_in, 16 * 4)
                    pe.matmul(out[:, 0:P], u_pool[:, 0, ch], pool_ctx[:, g, :], start=True, stop=True,
                              skip_group_check=True)
                    pe.matmul(out[:, P:2 * P], u_pool[:, 1, ch], pool_own[:, 0, g, :], start=False, stop=True,
                              skip_group_check=True)
                    pe.matmul(out[:, 2 * P:NT], u_pool[:, 2, ch], pool_own[:, 1, g, :], start=False, stop=True,
                              skip_group_check=True)
                    pe.matmul(out[:, 2 * P:2 * P + 8], u_pool[:, 1, ch], pool_cross[:, 0, g, :],
                              start=False, stop=True, skip_group_check=True)
                    last = pe.matmul(out[:, 2 * P - 8:2 * P], u_pool[:, 2, ch], pool_cross[:, 1, g, :],
                                     start=False, stop=True, skip_group_check=True)
                elif what == "pool_mix":
                    g, part = e[1:]
                    pe.wait_ge(pool_w_in[g % 2], 16 * (g // 2 + 1))
                    for j in range(2):
                        wait_free(pe, "pool", g, j)
                    for i, t in enumerate((0, 1) if part == 0 else (2,)):
                        for j in range(2):
                            last = pe.matmul(out[:, i * GROUP:(i + 1) * GROUP],
                                             pooled[:, 2 * g + j, t * P:(t + 1) * P],
                                             pool_w_sb[:, g % 2, j, :], start=j == 0, stop=j == 1)
                elif what == "mix":
                    c, t = e[1:]
                    pe.wait_ge(vn_ready, TOKS * NTH[c] + t + 1)
                    for i in range(2):
                        last = pe.matmul(out[:, i * GROUP:(i + 1) * GROUP], sgu_w_sb[:, 2 * NTH[c] + i, :],
                                         v_normed[:, t, i * GROUP:(i + 1) * GROUP], start=True, stop=True)
                filled(last, e)

            for p in places():
                if p[0] == "at":
                    k_step(p[1], p[2])
                for e in table.get(p, ()):
                    if e[0] in SIDE:
                        side_product(e)

        @block.scalar
        def _(act):
            own = [0]

            def then_own(ins):
                own[0] += 1
                ins.then_inc(act_own, 1)
                act.wait_ge(act_own, own[0])

            def round_half(half):
                wait_load(act, "mm", half // 2)
                if half >= WRING:
                    act.wait_ge(mm_done, half - WRING + 1)
                n = nth_load["mm", half // 2]
                src = raw[:, n % RAW, (half % 2) * 2 * CW:(half % 2 + 1) * 2 * CW]
                act.activation(w_hi[:, half % WRING, :, :].rearrange("p k n -> p (k n)"), src, ACT.Copy)\
                    .then_inc(hi_ready, 1)

            def norm_x(layer):
                for t in range(TOKS):
                    if layer == 0:
                        if t == 0:
                            act.wait_ge(x_in, 16 * TOKS)
                    else:
                        act.wait_ge(x_ready, PIECES * (t + 1))
                    act.activation(mixed[:, t, :], x[:, t, :], ACT.Square, accum_out=stat[:, 4, t:t + 1])\
                        .then_inc(x_squared, 1)
                act.wait_ge(x_mean, layer + 1)
                act.activation(stat[:, 6, :], stat[:, 5, :], ACT.Sqrt).then_inc(x_root, 1)

            def norm_piece(layer, j):
                act.wait_ge(x_scale, layer + 1)
                cols = slice(j * PIECE, (j + 1) * PIECE)
                act.activation(mixed[:, TOKS - 1, cols], x[:, TOKS - 1, cols], ACT.Copy,
                               scale=stat[:, 7, TOKS - 1:TOKS]).then_inc(xn_act, 1)

            def residual_root(layer):
                act.wait_ge(y_mean, layer + 1)
                act.activation(stat[:, 2, :], stat[:, 1, :], ACT.Sqrt).then_inc(y_root, 1)

            def square_y(c, t):
                n = TOKS * nth_out[c] + t
                j = CHUNKS[c][2] // CW
                if n:
                    act.wait_ge(y_squared, n)
                if c in (L1 - 1, 2 * L1 - 1) and t == 0:
                    then_own(act.activation(junk[:, 0:TOKS], stat[:, 6, :], ACT.Sqrt))
                wait_chunk(act, c)
                act.activation(junk[:, :], acc(c, t)[:, :], ACT.Square, accum_out=sq[:, t, j:j + 1])\
                    .then_inc(y_squared, 1)

            def part(e):
                what = e[0]
                if what == "cols":
                    wait_full(act, *e)
                    dst = scale_t if e[1] == SCALE_BLOCK else shift_t
                    freed(act.activation(dst[:, :, :].rearrange("p (j i) c -> p i j c", i=4),
                                         side_bank(e)[:, :].rearrange("p (i j n) -> p i j n", i=4, j=4)[:, :, :, 0:2],
                                         ACT.Copy), e)
                elif what == "h":
                    layer, k = e[1:]
                    if layer == 0:
                        act.wait_ge(first_ready, 2 * (k // 4 + 1))
                    elif k == 0:
                        wait_free(act, "cols", SCALE_BLOCK)
                        wait_free(act, "cols", SHIFT_BLOCK)
                    wait_full(act, *e)
                    for c_, lo_, hi_ in ((0, 0, P), (1, P, NT)):
                        last = act.activation(h_op[:, 0, k, lo_:hi_], side_bank(e)[:, lo_:hi_], ACT.Identity,
                                              bias=shift_t[:, k, c_:c_ + 1], scale=scale_t[:, k, c_:c_ + 1])
                    last.then_inc(op_hi, 1)
                elif what == "o":
                    layer, k = e[1:]
                    wait_full(act, *e)
                    dst = (o_low if k < 8 else h_op)[:, 0, k, :]
                    act.activation(dst, side_bank(e)[:, 0:NT], ACT.Copy).then_inc(op_hi, 1)
                elif what == "turn":
                    c, t = e[1:]
                    wait_full(act, *e)
                    h0 = HEADS if CHUNKS[c][1] == "k" else 4 * NTH[c]
                    freed(act.activation(qk_t[:, h0:h0 + 4, t * P:(t + 1) * P],
                                         side_bank(e)[:, :].rearrange("p (h n) -> p h n", h=4), ACT.Copy), e)
                elif what == "turn_p":
                    n = P if units[e[1]][1] == 0 else NT
                    wait_full(act, *e)
                    freed(act.activation(probs_t[:, 0:n], side_bank(e)[:, 0:n], ACT.Copy), e)
                elif what == "scores":
                    u = e[1]
                    n = P if units[u][1] == 0 else NT
                    act.wait_ge(neg_max_ready, u + 1)
                    freed(act.activation(probs[:, 0:n], side_bank(e)[:, 0:n], ACT.Exp, bias=neg_max[:, u:u + 1],
                                         scale=SCALE, accum_out=row_sum[:, u:u + 1]), e)
                elif what == "denominator":
                    g = e[1]
                    act.wait_ge(sink_shifted, g + 1)
                    act.activation(sink_exp[:, 12 * g:12 * g + 12], inv_sum[:, 12 * g:12 * g + 12], ACT.Exp)\
                        .then_inc(sink_exped, 1)
                elif what == "evac":
                    c, t = e[1:]
                    kind = CHUNKS[c][1]
                    src = acc(c, t)[:, :]
                    if kind in GATED:
                        wait_chunk(act, c)
                        n = nth_gate[c, t]
                        if n >= 2:
                            wait_acc(act, *gate_chunks[n - 2])
                        if n == 0:
                            act.wait_ge(roped_ready, len(nth_roped))
                        if CHUNKS[c][0] == 1 and CHUNKS[gate_chunks[n - 1][0]][0] == 0:
                            wait_free(act, "h", 1, KT - 1)
                        act.activation(silu[:, n % 2, :], src, ACT.Silu).then_inc(silu_ready, 1)
                    elif kind == "out":
                        square_y(c, t)
                    elif kind in ("v", "ub", "uc"):
                        wait_chunk(act, c)
                        if kind == "ub" and t == 0:
                            wait_full(act, "pv", len(units) - 1)
                            act.wait_ge(v_stored, 16)
                        dst = u_pool[:, t, NTH[c] * CW:(NTH[c] + 1) * CW] if kind == "uc" else v_nat[:, t, :]
                        act.activation(dst, src, ACT.Copy).then_inc(acc_free[c % 2], 1)
                    elif kind == "vd":
                        n = TOKS * NTH[c] + t
                        act.wait_ge(ln_var_ready, n + 1)
                        act.activation(ln_std[:, :], ln_mv[:, :, 1], ACT.Sqrt).then_inc(ln_root, 1)
                elif what in ("dft_ctx", "dft_lat"):
                    wait_full(act, *e)
                    dst, n = (dft_c, 256) if what == "dft_ctx" else (dft_l, CW)
                    freed(act.activation(dst[:, :], side_bank(e)[:, 0:n], ACT.Copy), e)
                elif what == "pool":
                    g, j = e[1:]
                    wait_full(act, *e)
                    freed(act.activation(pooled[:, 2 * g + j, :], side_bank(e)[:, 0:NT], ACT.Copy), e)
                elif what == "mix":
                    c, t = e[1:]
                    wait_full(act, *e)
                    for i in range(2):
                        h = 2 * NTH[c] + i
                        last = act.activation(mixed[:, t, 1024 + h * GROUP:1024 + (h + 1) * GROUP],
                                              side_bank(e)[:, i * GROUP:(i + 1) * GROUP], ACT.Identity,
                                              bias=sgu_b_sb[:, h:h + 1], scale=1.0)
                    freed(last, e)
                elif what == "gate_y":
                    c, n_cond = e[1:]
                    if n_cond == 0:
                        wait_acc(act, c - 1, TOKS - 1)
                    wait_full(act, *e)
                    freed(act.activation(silu[:, n_cond, :], side_bank(e)[:, :], ACT.Copy), e)
                elif what == "first_weights":
                    round_half(0)
                    round_half(1)
                elif what == "xn":
                    norm_piece(*e[1:])
                elif what == "residual":
                    residual_root(e[1])
                    if e[1] == 0:
                        norm_x(1)

            act.dma_start(cond_in[:, :, :], cond_cols).then_inc(cond_landed, 16)
            for t in range(TOKS):
                src = x_prompt[0] if t == 0 else x_sample[0, (t - 1) * P:t * P, :]
                act.dma_start(x[:, t, :], src).then_inc(x_in, 16)
            act.wait_ge(cond_landed, 16)
            act.wait_ge(cleared, 1)
            for i in range(2):
                act.activation(cond[:, :, 2 * i:2 * i + 2], cond_in[:, :, :], ACT.Silu).then_inc(cond_ready, 1)
            norm_x(0)
            for j in range(PIECES):
                norm_piece(0, j)
            act.wait_ge(const_in, 48)
            act.activation(row_sel_r[:, :, :], row_sel[:, :, :], ACT.Copy).then_inc(rows_selectable, 1)
            for p in places():
                ahead = half_ahead(p)
                if ahead is not None and p[1] in (0, 1):
                    round_half(ahead)
                for e in table.get(p, ()):
                    part(e)
                if ahead is not None and p[1] not in (0, 1):
                    round_half(ahead)

        @block.vector
        def _(dve):
            own = [0]

            def then_own(ins):
                own[0] += 1
                ins.then_inc(dve_own, 1)
                dve.wait_ge(dve_own, own[0])

            def split_half(half):
                dve.wait_ge(hi_ready, half + 1)
                n = nth_load["mm", half // 2]
                src = raw[:, n % RAW, (half % 2) * 2 * CW:(half % 2 + 1) * 2 * CW]
                hi = w_hi[:, half % WRING, :, :].rearrange("p k n -> p (k n)").bitcast(F32)
                dve.tensor_tensor(w_lo[:, half % WRING, :, :].rearrange("p k n -> p (k n)"), src, hi, ALU.subtract)\
                    .then_inc(lo_ready, 1)

            def finish_rows(m, dst):
                if m == SHIFT_BLOCK:
                    return
                dve.wait_ge(weight_in, 16 * (NORM_BLOCKS.index(m) + 1))
                last = dve.scalar_tensor_tensor(out=dst[:, :], in0=dst[:, :], scalar=1.0 if m == SCALE_BLOCK else 0.0,
                                                in1=weight_rows[:, :], op0=ALU.add, op1=ALU.mult)
                if m in GATE_BLOCK:
                    then_own(last)
                    dve.wait_ge(const_in, 48)
                    then_own(dve.tensor_copy(gate_parts[:, :], dst[:, :]))
                    last = dve.scalar_tensor_tensor(out=gate_parts[:, :], in0=gate_parts[:, :].bitcast(F32),
                                                    scalar=minus_lo[:, 0:1], in1=dst[:, :],
                                                    op0=ALU.mult, op1=ALU.add)
                last.then_inc(rows_done, 1)

            def norm_x(layer):
                dve.wait_ge(x_squared, TOKS * (layer + 1))
                dve.tensor_scalar(stat[:, 5, :], stat[:, 4, :], 1.0 / D, EPS, ALU.mult, ALU.add).then_inc(x_mean, 1)
                dve.wait_ge(x_root, layer + 1)
                dve.reciprocal(stat[:, 7, :], stat[:, 6, :]).then_inc(x_scale, 1)
                dve.wait_ge(x_scale, layer + 1)

            def norm_piece(j):
                cols = slice(j * PIECE, (j + 1) * PIECE)
                for t in range(TOKS - 1):
                    dve.tensor_scalar(mixed[:, t, cols], x[:, t, cols], stat[:, 7, t:t + 1], None, ALU.mult)\
                        .then_inc(xn_ready, 1)

            def residual(layer):
                dve.wait_ge(y_squared, TOKS * N_OUT * (layer + 1))
                then_own(dve.tensor_reduce(stat[:, 0, :], sq[:, :, :], AX.X, ALU.add))
                dve.tensor_scalar(stat[:, 1, :], stat[:, 0, :], 1.0 / D, EPS, ALU.mult, ALU.add).then_inc(y_mean, 1)
                dve.wait_ge(y_root, layer + 1)
                then_own(dve.reciprocal(stat[:, 3, :], stat[:, 2, :]))
                wait_acc(dve, layer * L1 + L1 - 1, TOKS - 1)
                for t in range(TOKS):
                    for j in range(PIECES):
                        cols = slice(j * PIECE, (j + 1) * PIECE)
                        dve.scalar_tensor_tensor(out=x[:, t, cols], in0=mixed[:, t, cols], scalar=stat[:, 3, t:t + 1],
                                                 in1=x[:, t, cols], op0=ALU.mult, op1=ALU.add).then_inc(x_ready, 1)

            def rotate(c, t):
                n = nth_roped[c, t]
                src = acc(c, t)
                if n:
                    prev = next(ct for ct, i in nth_roped.items() if i == n - 1)
                    wait_full(dve, "turn", *prev)
                if n == 1:
                    dve.wait_ge(k_stored, 16)
                    wait_free(dve, "h", 0, KT - 1)
                if t == 0:
                    dve.tensor_copy(roped[:, :], src[:, :]).then_inc(roped_ready, 1)
                    return
                dve.wait_ge(attn_in, 16 * 5)
                a = "p (h a b f) -> p h a b f"
                s4 = src[:, :].rearrange(a, h=4, a=2, b=2)
                tmp4 = rope_tmp.rearrange(a, h=4, a=2, b=2)
                sin = rope_sb[:, 1, t - 1, :].rearrange("p (a b f) -> p a b f", a=2, b=2)
                cos = rope_sb[:, 0, t - 1, :].unsqueeze(1).to_broadcast([P, 4, P])
                if n > 1:
                    dve.wait_ge(roped_ready, n)
                for b in range(2):
                    dve.tensor_tensor(tmp4[:, :, :, b, :], s4[:, :, :, 1 - b, :],
                                      sin[:, :, b, :].unsqueeze(1).to_broadcast([P, 4, 2, 32]), ALU.mult)
                then_own(dve.tensor_tensor(roped[:, :].rearrange("p (h d) -> p h d", h=4),
                                           src[:, :].rearrange("p (h d) -> p h d", h=4), cos, ALU.mult))
                dve.tensor_tensor(roped[:, :], roped[:, :], rope_tmp, ALU.add).then_inc(roped_ready, 1)

            def part(e):
                what = e[0]
                if what == "first_ada":
                    b, w, i = e[1:]
                    dst = (rows, gate)[w]
                    wait_full(dve, *e)
                    if i == 0:
                        if b:
                            wait_full(dve, "first_cols", b - 1, w)
                        freed(dve.tensor_copy(dst[:, :], side_bank(e)[:, :]), e)
                    else:
                        wait_free(dve, "first_ada", b, w, i - 1)
                        freed(dve.tensor_tensor(dst[:, :], side_bank(e)[:, :], dst[:, :], ALU.add), e)
                elif what == "first_cols":
                    b, w = e[1:]
                    ks = slice(4 * b, 4 * b + 4)

                    def both(row):
                        return first_c[:, row, ks].unsqueeze(2).to_broadcast([P, 4, 2])

                    wait_full(dve, *e)
                    if b:
                        dve.wait_ge(first_ready, 2 * b)
                    freed(dve.tensor_reduce(col_sum[:, w, :, :],
                                            side_bank(e)[:, :].rearrange("p (i j n) -> p i n j", i=4, j=4)[:, :, 0:2, :],
                                            AX.X, ALU.add), e)
                    wait_free(dve, *e)
                    dve.wait_ge(first_in, 16)
                    if w == 0:
                        then_own(dve.tensor_tensor(col_sum[:, 0, :, :], col_sum[:, 0, :, :], both(0), ALU.add))
                        dve.scalar_tensor_tensor(out=scale_t[:, ks, :], in0=col_sum[:, 0, :, :], scalar=1.0,
                                                 in1=both(2), op0=ALU.add, op1=ALU.mult).then_inc(first_ready, 1)
                    else:
                        dve.tensor_tensor(shift_t[:, ks, :], col_sum[:, 1, :, :], both(1), ALU.add)\
                            .then_inc(first_ready, 1)
                elif what == "ada":
                    m, k, n = e[1:]
                    dst = gate if m in GATE_BLOCK else rows
                    wait_full(dve, *e)
                    if k == 0:
                        dve.wait_ge(bias_in, 16 * (m + 1))
                        wait_full(dve, *{0: ("first_cols", 3, 1), 1: ("first_cols", 3, 0),
                                         2: ("cols", SCALE_BLOCK), 3: ("gate_y", L1 - 1, 1)}[m])
                        freed(dve.tensor_tensor(dst[:, :], side_bank(e)[:, :], bias_rows[:, :], ALU.add), e)
                    else:
                        wait_free(dve, *ada_entry[m, k - 1])
                        freed(dve.tensor_tensor(dst[:, :], side_bank(e)[:, :], dst[:, :], ALU.add), e)
                    if k + n == KT:
                        wait_free(dve, *e)
                        finish_rows(m, dst)
                elif what == "h":
                    layer, k = e[1:]
                    if layer == 0:
                        dve.wait_ge(first_ready, 2 * (k // 4 + 1))
                    elif k == 0:
                        wait_free(dve, "cols", SCALE_BLOCK)
                        wait_free(dve, "cols", SHIFT_BLOCK)
                        wait_acc(dve, L1 - 1, TOKS - 1)
                    if k:
                        wait_free(dve, "h", layer, k - 1)
                    dve.wait_ge(op_hi, nth_op("h", layer, k) + 1)
                    for c_, lo_, hi_ in ((0, 0, P), (1, P, NT)):
                        last = dve.tensor_scalar(h_tmp[:, lo_:hi_], side_bank(e)[:, lo_:hi_],
                                                 scale_t[:, k, c_:c_ + 1], shift_t[:, k, c_:c_ + 1],
                                                 ALU.mult, ALU.add)
                    then_own(last)
                    freed(dve.tensor_tensor(h_op[:, 1, k, :], h_tmp, h_op[:, 0, k, :].bitcast(F32), ALU.subtract), e)
                elif what == "o":
                    layer, k = e[1:]
                    dst = o_low if k < 8 else h_op
                    dve.wait_ge(op_hi, nth_op("o", layer, k) + 1)
                    freed(dve.tensor_tensor(dst[:, 1, k, :], side_bank(e)[:, 0:NT], dst[:, 0, k, :].bitcast(F32),
                                            ALU.subtract), e)
                elif what == "scores":
                    u = e[1]
                    t = units[u][1]
                    n = P if t == 0 else NT
                    s = side_bank(e)
                    wait_full(dve, *e)
                    if u == 0:
                        dve.wait_ge(attn_in, 16 * 5)
                        then_own(dve.tensor_scalar(neg_sinks[:, :], sinks[:, :], -1.0, None, ALU.mult))
                    if t:
                        other = slice((2 - t) * P, (3 - t) * P)
                        then_own(dve.tensor_tensor(s[:, other], s[:, other], mask_sb[:, t - 1, :], ALU.add))
                    then_own(dve.tensor_reduce(row_max[:, u:u + 1], s[:, 0:n], AX.X, ALU.max))
                    dve.tensor_scalar(neg_max[:, u:u + 1], row_max[:, u:u + 1], -SCALE, neg_sinks[:, u:u + 1],
                                      ALU.mult, ALU.min).then_inc(neg_max_ready, 1)
                elif what == "pv":
                    g, t, i = units[e[1]]
                    h = 4 * g + i
                    wait_full(dve, *e)
                    freed(dve.tensor_copy(mixed[:, t, h * HD:(h + 1) * HD], side_bank(e)[:, 0:HD]), e)
                elif what == "denominator":
                    g = e[1]
                    s = slice(12 * g, 12 * g + 12)
                    dve.wait_ge(neg_max_ready, 12 * (g + 1))
                    dve.tensor_tensor(inv_sum[:, s], sinks[:, s], neg_max[:, s], ALU.add).then_inc(sink_shifted, 1)
                    dve.wait_ge(sink_exped, g + 1)
                    then_own(dve.tensor_tensor(sink_exp[:, s], sink_exp[:, s], row_sum[:, s], ALU.add))
                    dve.reciprocal(inv_sum[:, s], sink_exp[:, s]).then_inc(inv_ready, 1)
                elif what == "evac":
                    c, t = e[1:]
                    kind = CHUNKS[c][1]
                    src = acc(c, t)
                    if kind in ROPED:
                        wait_chunk(dve, c)
                        rotate(c, t)
                    elif kind in GATED:
                        n = nth_gate[c, t]
                        dve.wait_ge(silu_ready, n + 1)
                        g_sb = silu[:, n % 2, :]
                        col = GATED[kind] + CW * NTH[c]
                        if kind == "ga":
                            g = NTH[c]
                            dve.wait_ge(inv_ready, g + 1)
                            if t == 0:
                                wait_free(dve, "pv", 12 * g + 11)
                            for i in range(4):
                                u = 12 * g + 4 * t + i
                                o = mixed[:, t, col + i * HD:col + (i + 1) * HD]
                                last = dve.scalar_tensor_tensor(out=o, in0=o, scalar=inv_sum[:, u:u + 1],
                                                                in1=g_sb[:, i * HD:(i + 1) * HD],
                                                                op0=ALU.mult, op1=ALU.mult)
                            last.then_inc(acc_free[c % 2], 1)
                        else:
                            if kind == "gb" and t == 0:
                                wait_free(dve, "dft_ch", 3)
                            if kind == "gc" and t == 0:
                                for g in (2 * NTH[c], 2 * NTH[c] + 1):
                                    for part_ in range(2):
                                        wait_free(dve, "pool_mix", g, part_)
                            if kind == "gd":
                                wait_acc(dve, c - 2, t)
                            o = mixed[:, t, col:col + CW]
                            dve.tensor_tensor(o, o, g_sb, ALU.mult).then_inc(acc_free[c % 2], 1)
                    elif kind == "out":
                        dve.wait_ge(y_squared, TOKS * nth_out[c] + t + 1)
                        n_cond = min(t, 1)
                        wait_free(dve, "gate_y", c, n_cond)
                        col = CHUNKS[c][2]
                        dve.tensor_tensor(mixed[:, t, col:col + CW], src[:, :], silu[:, n_cond, :], ALU.mult)\
                            .then_inc(acc_free[c % 2], 1)
                    elif kind == "vd":
                        n = TOKS * NTH[c] + t
                        wait_chunk(dve, c)
                        if n:
                            dve.wait_ge(vn_ready, n)
                        for i in range(2):
                            last = dve.bn_stats(ln_stats[:, i, :], src[:, i * GROUP:(i + 1) * GROUP])
                        then_own(last)
                        for i in range(2):
                            last = dve.bn_aggr(ln_mv[:, i, :], ln_stats[:, i, :])
                        then_own(last)
                        dve.tensor_scalar(ln_mv[:, :, 1], ln_mv[:, :, 1], EPS, None, ALU.add).then_inc(ln_var_ready, 1)
                    elif kind == "ud":
                        wait_chunk(dve, c)
                        wait_free(dve, "mix", vd_chunks[NTH[c]], t)
                        o = mixed[:, t, 1024 + CW * NTH[c]:1024 + CW * (NTH[c] + 1)]
                        dve.tensor_tensor(o, o, src[:, :], ALU.mult).then_inc(acc_free[c % 2], 1)
                elif what == "evac2":
                    c, t = e[1:]
                    n = TOKS * NTH[c] + t
                    src = acc(c, t)
                    dve.wait_ge(ln_root, n + 1)
                    then_own(dve.reciprocal(ln_std[:, :], ln_std[:, :]))
                    dve.wait_ge(sgu_in, 16)
                    if NTH[c]:
                        wait_full(dve, "mix", vd_chunks[0], t)
                    col = CW * NTH[c]
                    for i in range(2):
                        o = v_normed[:, t, i * GROUP:(i + 1) * GROUP]
                        last = dve.scalar_tensor_tensor(
                            out=o, in0=src[:, i * GROUP:(i + 1) * GROUP], scalar=ln_mv[:, i, 0:1],
                            in1=sgu_n[:, col + i * GROUP:col + (i + 1) * GROUP], op0=ALU.subtract, op1=ALU.mult)
                    last.then_inc(acc_free[c % 2], 1)
                    wait_acc(dve, c, t)
                    for i in range(2):
                        o = v_normed[:, t, i * GROUP:(i + 1) * GROUP]
                        last = dve.tensor_scalar(o, o, ln_std[:, i:i + 1], None, ALU.mult)
                    last.then_inc(vn_ready, 1)
                elif what == "dft_ch":
                    g = e[1]
                    wait_full(dve, *e)
                    freed(dve.tensor_copy(mixed[:, :, ATT + g * P:ATT + (g + 1) * P],
                                          side_bank(e)[:, 0:NT].rearrange("p (t n) -> p t n", t=TOKS)), e)
                elif what == "pool_mix":
                    g, part_ = e[1:]
                    wait_full(dve, *e)
                    toks = (0, 1) if part_ == 0 else (2,)
                    for i, t in enumerate(toks):
                        last = dve.tensor_tensor(mixed[:, t, g * GROUP:(g + 1) * GROUP],
                                                 side_bank(e)[:, i * GROUP:(i + 1) * GROUP],
                                                 pool_s[:, g * GROUP:(g + 1) * GROUP], ALU.mult)
                    freed(last, e)
                elif what == "xn":
                    norm_piece(e[2])
                elif what == "residual":
                    residual(e[1])
                    if e[1] == 0:
                        norm_x(1)
                elif what == "first_weights":
                    split_half(0)
                    split_half(1)
                elif what == "norm":
                    norm_x(0)
                    for j in range(PIECES):
                        norm_piece(j)

            for p in places():
                ahead = half_ahead(p)
                if ahead is not None and p[1] in (0, 1):
                    split_half(ahead)
                for e in table.get(p, ()):
                    part(e)
                if ahead is not None and p[1] not in (0, 1):
                    split_half(ahead)


def shape_constants():
    import numpy as np
    identity = np.eye(P, dtype=np.float32)
    row_select = np.zeros((P, 2, P), np.float32)
    minus_lo = np.zeros((P, 1), np.float32)
    for j in range(4):
        for cond in range(2):
            row_select[32 * j + cond, cond, :] = 1.0
            row_select[32 * j + 2 + cond, cond, :] = 1.0
            minus_lo[32 * j + 2 + cond] = -1.0
    n_freq = HD // 4
    inv = (np.float32(10000.0) ** (-np.arange(n_freq, dtype=np.float32) / np.float32(n_freq))).astype(np.float32)
    pos = np.arange(2 * P)
    angle = np.stack([(pos // 64)[:, None].astype(np.float32) * inv,
                      (pos % 64)[:, None].astype(np.float32) * inv], axis=1)
    cos = np.repeat(np.cos(angle)[:, :, None, :], 2, axis=2)
    sin = np.stack([-np.sin(angle), np.sin(angle)], axis=2)
    rope = np.stack([cos.reshape(2, P, HD), sin.reshape(2, P, HD)]).transpose(2, 0, 1, 3)
    i, j = np.arange(P)[:, None], np.arange(P)[None, :]
    mask = np.stack([np.where(j <= i, 0.0, -1e30), np.where(i <= j, 0.0, -1e30)], axis=1)

    def cos_sin(n):
        a = 2 * np.pi * (np.outer(np.arange(n), np.arange(n)) % n) / n
        return np.cos(a) / np.sqrt(n), np.sin(a) / np.sqrt(n)

    c128, s128 = cos_sin(P)
    c256, s256 = cos_sin(2 * P)
    both = np.concatenate([c256, s256], axis=1).reshape(2, P, 4 * P).transpose(1, 0, 2).reshape(P, 8 * P)
    dft = np.concatenate([c128, s128, both, c128, -s128], axis=1)

    def pool(length, window):
        at = np.arange(length)
        lo, hi = np.clip(at - window // 2, 0, length), np.clip(at + window // 2, 0, length)
        src = np.arange(length)[:, None]
        return ((src >= lo) & (src < hi)) / (hi - lo) - (src == at)

    ctx = np.stack([pool(P, w) for w in WINDOWS], axis=1)
    lat = np.stack([pool(2 * P, w) for w in WINDOWS], axis=1)
    own = np.stack([lat[:P, :, :P], lat[P:, :, P:]], axis=1)
    cross = np.stack([lat[:P, :, P:P + 8], lat[P:, :, P - 8:P]], axis=1)
    pool_mats = np.concatenate([ctx.reshape(P, -1), own.reshape(P, -1), cross.reshape(P, -1)], axis=1)
    return {name: np.ascontiguousarray(a, dtype=np.float32) for name, a in {
        "identity": identity, "row_select": row_select, "minus_lo_rows": minus_lo, "rope": rope, "window_mask": mask,
        "dft": dft, "pool_mats": pool_mats}.items()}


def kernel(x_prompt, x_sample, cache_k, cache_v, c, c_ctx, w_ada, b_ada, norm_pre, norm_post, w_in, w_out,
           attn_sink, pool_w, pool_scale, sgu_norm, sgu_w, sgu_b):
    import numpy as np
    import concourse.bacc as bacc
    from concourse.bass_utils import run_bass_kernel_spmd

    def spread(row):
        out = np.zeros((P, CW), np.float32)
        for j in range(4):
            for cond in range(2):
                out[32 * j + cond] = out[32 * j + 2 + cond] = row[CW * j:CW * (j + 1)]
        return out

    a = {name: np.asarray(v) for name, v in dict(
        x_prompt=x_prompt, x_sample=x_sample, cache_k=cache_k, cache_v=cache_v, c=c, c_ctx=c_ctx, w_ada=w_ada,
        b_ada=b_ada, norm_pre=norm_pre, norm_post=norm_post, w_in=w_in, w_out=w_out, attn_sink=attn_sink,
        pool_w=pool_w, pool_scale=pool_scale, sgu_norm=sgu_norm, sgu_w=sgu_w, sgu_b=sgu_b).items()}
    arrays = {
        "x_prompt": a["x_prompt"], "x_sample": a["x_sample"],
        "cond_cols": np.stack([a["c_ctx"], a["c"][0]]).reshape(2, KT, P).transpose(2, 1, 0),
        "w_ada": a["w_ada"],
        "first_cols": np.stack([a["b_ada"][0, D * SCALE_COL:D * (SCALE_COL + 1)],
                                a["b_ada"][0, D * SHIFT_COL:D * (SHIFT_COL + 1)],
                                a["norm_pre"][0]]).reshape(3, KT, P).transpose(2, 0, 1),
        "ada_rows": np.stack([spread(a["b_ada"][layer, D * third:D * (third + 1)]) for layer, third in BLOCKS]),
        "norm_rows": np.stack([spread(a["norm_pre" if m == SCALE_BLOCK else "norm_post"][BLOCKS[m][0]])
                               for m in NORM_BLOCKS]),
        "w_in": a["w_in"], "w_out": a["w_out"],
        "cache_kt": a["cache_k"][0, 0].transpose(2, 1, 0),
        "cache_v": a["cache_v"][0, 0].reshape(P, CW),
        "sink_units": np.stack([a["attn_sink"][0, 4 * g + i] for g, _, i in head_units()]).reshape(1, 36),
        "pool_w": a["pool_w"], "pool_scale": a["pool_scale"], "sgu_norm": a["sgu_norm"],
        "sgu_wt": a["sgu_w"][0].transpose(2, 0, 1), "sgu_bt": a["sgu_b"][0].transpose(1, 0),
        **shape_constants(),
    }
    outs = {"y_prompt": (1, P, D), "y_sample": (1, 2 * P, D), "new_k": (P, CW), "new_v": (P, CW)}
    nc = bacc.Bacc("TRN2", target_bir_lowering=False, num_devices=1)
    feed, aps = {}, {}
    for name, v in arrays.items():
        v = np.ascontiguousarray(v)
        feed[f"in_{name}"] = v
        aps[name] = nc.dram_tensor(f"in_{name}", v.shape, mybir.dt.from_np(v.dtype), kind="ExternalInput").ap()
    for name, shape in outs.items():
        aps[name] = nc.dram_tensor(f"out_{name}", shape, F32, kind="ExternalOutput").ap()
    hybrid_step(nc, **aps)
    got = run_bass_kernel_spmd(nc, [feed], core_ids=[0]).results[0]
    cache_shape = (1, 1, P, KV_HEADS, HD)
    return (got["out_y_prompt"], got["out_y_sample"], got["out_new_k"].reshape(cache_shape),
            got["out_new_v"].reshape(cache_shape))
```
